# Optimizing a Trainium2 kernel written in Bass

```python
import jax, jax.numpy as jnp
from jax import lax
import numpy as np

D_MODEL = 1024
BATCH = 1
SEQ = 512
DEPTH = 1

CHUNK = 64
Q_BLOCK = 64
ROPE_THETA = 500000.0
EPS = 1e-6

A_HEADS = 8
A_HEAD_DIM = 64
A_WIDTH = A_HEADS * A_HEAD_DIM
IDX_HEADS = 16
IDX_DIM = 64
TOPK_MAX = 256

B_HEADS = 4
B_HEAD_DIM = 128
B_WIDTH = B_HEADS * B_HEAD_DIM
CONV_WIDTH = 4

IN_SIZES = (
    A_WIDTH, A_WIDTH, A_WIDTH, A_WIDTH,
    IDX_HEADS * IDX_DIM, IDX_DIM, IDX_HEADS,
    B_WIDTH, B_WIDTH, B_WIDTH, B_WIDTH, B_WIDTH,
    B_HEADS, B_HEADS,
    D_MODEL, D_MODEL,
)
N_IN = sum(IN_SIZES)

kernel_name = 'hybrid_dsa_mlstm_gated_merge'

def rmsnorm(x, g):
    x32 = x.astype(jnp.float32)
    y = x32 * lax.rsqrt(jnp.mean(x32 * x32, axis=-1, keepdims=True) + EPS)
    return (y * g.astype(jnp.float32)).astype(x.dtype)

def head_norm(x, g):
    shp = x.shape
    x32 = x.astype(jnp.float32).reshape(shp[:-1] + (B_HEADS, B_HEAD_DIM))
    mu = jnp.mean(x32, axis=-1, keepdims=True)
    var = jnp.mean(jnp.square(x32 - mu), axis=-1, keepdims=True)
    y = ((x32 - mu) * lax.rsqrt(var + EPS)).reshape(shp)
    return (y * g.astype(jnp.float32)).astype(x.dtype)

def partial_rope(x, pos):
    d = x.shape[-1]
    rd = d // 4
    half = rd // 2
    inv = ROPE_THETA ** (-(jnp.arange(half, dtype=jnp.float32) * 2.0 / rd))
    ang = pos.astype(jnp.float32)[:, None] * inv[None, :]
    cos = jnp.cos(ang)[:, None, :]
    sin = jnp.sin(ang)[:, None, :]
    x32 = x.astype(jnp.float32)
    x1, x2, rest = x32[..., :half], x32[..., half:rd], x32[..., rd:]
    out = jnp.concatenate([x1 * cos - x2 * sin, x1 * sin + x2 * cos, rest], axis=-1)
    return out.astype(x.dtype)

def causal_conv(u, w, b):
    K = w.shape[0]
    S = u.shape[1]
    up = jnp.pad(u, ((0, 0), (K - 1, 0), (0, 0)))
    return sum(up[:, j:j + S] * w[j] for j in range(K)) + b

def dsa_attention(q, k, v, qi, ki, wi, k_sel):
    Bsz, S, H, Dh = q.shape
    nblk = S // Q_BLOCK
    kchunk = jnp.arange(S) // CHUNK
    ki32 = ki.astype(jnp.float32)

    def blocks(a):
        return jnp.moveaxis(a.reshape((Bsz, nblk, Q_BLOCK) + a.shape[2:]), 1, 0)

    qpos = jnp.arange(S).reshape(nblk, Q_BLOCK)

    def one_block(args):
        q_b, qi_b, wi_b, pos_b = args
        s_idx = jnp.einsum('bthd,bsd->bths', qi_b.astype(jnp.float32), ki32) * (IDX_DIM ** -0.5)
        score = jnp.einsum('bth,bths->bts', wi_b.astype(jnp.float32), jax.nn.relu(s_idx))
        qchunk = pos_b // CHUNK
        admissible = kchunk[None, :] <= qchunk[:, None]
        score = jnp.where(admissible[None], score, -jnp.inf)
        _, idx = lax.top_k(score, k_sel)
        valid = (idx // CHUNK) <= qchunk[None, :, None]
        k_g = jax.vmap(lambda kb, ib: kb[ib])(k, idx)
        v_g = jax.vmap(lambda vb, ib: vb[ib])(v, idx)
        logits = jnp.einsum('bthd,btjhd->bthj', q_b.astype(jnp.float32),
                            k_g.astype(jnp.float32)) * (Dh ** -0.5)
        logits = jnp.where(valid[:, :, None, :], logits, -jnp.inf)
        p = jax.nn.softmax(logits, axis=-1)
        out = jnp.einsum('bthj,btjhd->bthd', p, v_g.astype(jnp.float32))
        return out.astype(q.dtype)

    out = lax.map(one_block, (blocks(q), blocks(qi), blocks(wi), qpos))
    return jnp.moveaxis(out, 0, 1).reshape(Bsz, S, H * Dh)

def mlstm_chunkwise(q, k, v, log_i, log_f):
    Bsz, H, S, dk = q.shape
    dv = v.shape[-1]
    nc = S // CHUNK

    def to_chunks(a):
        a = a.astype(jnp.float32)
        return jnp.moveaxis(a.reshape((Bsz, H, nc, CHUNK) + a.shape[3:]), 2, 0)

    xs = (to_chunks(q), to_chunks(k), to_chunks(v), to_chunks(log_i), to_chunks(log_f))
    causal = jnp.tril(jnp.ones((CHUNK, CHUNK), dtype=bool))

    def step(carry, xc):
        C, n, m = carry
        qc, kc, vc, li, lf = xc
        b = jnp.cumsum(lf, axis=-1)
        D = jnp.where(causal, b[..., :, None] - b[..., None, :] + li[..., None, :], -jnp.inf)
        m_inter = b + m[..., None]
        m_t = jnp.maximum(m_inter, jnp.max(D, axis=-1))
        w_inter = jnp.exp(m_inter - m_t)
        P = jnp.exp(D - m_t[..., None])
        s_qk = jnp.einsum('bhtd,bhsd->bhts', qc, kc) * P
        num = (w_inter[..., None] * jnp.einsum('bhtd,bhde->bhte', qc, C)
               + jnp.einsum('bhts,bhse->bhte', s_qk, vc))
        den = w_inter * jnp.einsum('bhtd,bhd->bht', qc, n) + jnp.sum(s_qk, axis=-1)
        h = num / jnp.maximum(jnp.abs(den), jnp.exp(-m_t))[..., None]
        b_L = b[..., -1]
        g = b_L[..., None] - b + li
        m_new = jnp.maximum(b_L + m, jnp.max(g, axis=-1))
        decay = jnp.exp(b_L + m - m_new)
        wk = jnp.exp(g - m_new[..., None])
        C_new = decay[..., None, None] * C + jnp.einsum('bhs,bhsd,bhse->bhde', wk, kc, vc)
        n_new = decay[..., None] * n + jnp.einsum('bhs,bhsd->bhd', wk, kc)
        return (C_new, n_new, m_new), h

    init = (jnp.zeros((Bsz, H, dk, dv), jnp.float32),
            jnp.zeros((Bsz, H, dk), jnp.float32),
            jnp.zeros((Bsz, H), jnp.float32))
    _, hs = lax.scan(step, init, xs)
    return jnp.moveaxis(hs, 0, 2).reshape(Bsz, H, S, dv)

def setup_inputs(seed: int = 0) -> dict:
    key = jax.random.key(seed)
    ks = jax.random.split(key, 12)
    f32 = jnp.float32
    x = jax.random.normal(ks[0], (BATCH, SEQ, D_MODEL), f32)
    norm_g = 1.0 + 0.05 * jax.random.normal(ks[1], (DEPTH, D_MODEL), f32)
    w_in = jax.random.normal(ks[2], (DEPTH, D_MODEL, N_IN), f32) * D_MODEL ** -0.5
    conv_w = jax.random.normal(ks[3], (DEPTH, CONV_WIDTH, 2 * B_WIDTH), f32) * CONV_WIDTH ** -0.5
    conv_b = 0.02 * jax.random.normal(ks[4], (DEPTH, 2 * B_WIDTH), f32)
    b_igate = 0.1 * jax.random.normal(ks[5], (DEPTH, B_HEADS), f32)
    b_fgate = 3.0 + 3.0 * jax.random.uniform(ks[6], (DEPTH, B_HEADS), f32)
    head_norm_g = 1.0 + 0.05 * jax.random.normal(ks[7], (DEPTH, B_WIDTH), f32)
    w_branch_a = jax.random.normal(ks[8], (DEPTH, A_WIDTH, D_MODEL), f32) * A_WIDTH ** -0.5
    w_branch_b = jax.random.normal(ks[9], (DEPTH, B_WIDTH, D_MODEL), f32) * B_WIDTH ** -0.5
    w_out = jax.random.normal(ks[10], (DEPTH, D_MODEL, D_MODEL), f32) * D_MODEL ** -0.5
    final_norm_g = 1.0 + 0.05 * jax.random.normal(ks[11], (D_MODEL,), f32)
    return {'x': x, 'norm_g': norm_g, 'w_in': w_in, 'conv_w': conv_w, 'conv_b': conv_b,
            'b_igate': b_igate, 'b_fgate': b_fgate, 'head_norm_g': head_norm_g,
            'w_branch_a': w_branch_a, 'w_branch_b': w_branch_b, 'w_out': w_out,
            'final_norm_g': final_norm_g}

def reference(x, norm_g, w_in, conv_w, conv_b, b_igate, b_fgate, head_norm_g,
              w_branch_a, w_branch_b, w_out, final_norm_g):
    Bsz, S, _ = x.shape
    pos = jnp.arange(S)
    k_sel = min(TOPK_MAX, S // 4)
    offsets = np.cumsum(IN_SIZES)[:-1]
    for l in range(DEPTH):
        h = rmsnorm(x, norm_g[l])
        (a_q, a_k, a_v, a_z, i_q, i_k, i_w,
         b_q, b_k, b_v, b_z, b_o, b_i, b_f, g_a, g_b) = jnp.split(h @ w_in[l], offsets, axis=-1)

        q_a = partial_rope(a_q.reshape(Bsz, S, A_HEADS, A_HEAD_DIM), pos)
        k_a = partial_rope(a_k.reshape(Bsz, S, A_HEADS, A_HEAD_DIM), pos)
        v_a = a_v.reshape(Bsz, S, A_HEADS, A_HEAD_DIM)
        q_i = partial_rope(i_q.reshape(Bsz, S, IDX_HEADS, IDX_DIM), pos)
        k_i = partial_rope(i_k[:, :, None, :], pos)[:, :, 0]
        w_i = i_w * IDX_HEADS ** -0.5
        o_a = dsa_attention(q_a, k_a, v_a, q_i, k_i, w_i, k_sel)
        y_a = (o_a * jax.nn.silu(a_z)) @ w_branch_a[l]

        qk_b = jax.nn.silu(causal_conv(jnp.concatenate([b_q, b_k], axis=-1), conv_w[l], conv_b[l]))
        q_b, k_b = jnp.split(qk_b, 2, axis=-1)

        def heads(t):
            return t.reshape(Bsz, S, B_HEADS, B_HEAD_DIM).transpose(0, 2, 1, 3)

        log_i = (b_i + b_igate[l]).astype(jnp.float32).transpose(0, 2, 1)
        log_f = jax.nn.log_sigmoid((b_f + b_fgate[l]).astype(jnp.float32)).transpose(0, 2, 1)
        cell = mlstm_chunkwise(heads(q_b), heads(k_b) * B_HEAD_DIM ** -0.5, heads(b_v), log_i, log_f)
        cell = cell.transpose(0, 2, 1, 3).reshape(Bsz, S, B_WIDTH).astype(x.dtype)
        h_b = head_norm(jax.nn.sigmoid(b_o) * cell, head_norm_g[l])
        y_b = (h_b * jax.nn.silu(b_z)) @ w_branch_b[l]

        merged = jax.nn.sigmoid(g_a) * y_a + jax.nn.sigmoid(g_b) * y_b
        x = x + merged @ w_out[l]
    return rmsnorm(x, final_norm_g)


_drawn_inputs = setup_inputs


def setup_inputs(seed=0):
    import zlib

    import numpy as np

    out = dict(_drawn_inputs(seed))
    spreads = {}
    factors = {'conv_b': 8.0, 'b_igate': 8.0, 'head_norm_g': 3.752}
    for name, (base, spread) in spreads.items():
        noise = np.random.default_rng([zlib.crc32(name.encode()), seed]).standard_normal(out[name].shape)
        drawn = base * np.exp(spread * noise) if base else spread * noise
        out[name] = __import__('jax').numpy.asarray(drawn.astype(out[name].dtype))
    for name, factor in factors.items():
        out[name] = (out[name] * factor).astype(out[name].dtype)
    return out
```

```python
from contextlib import ExitStack

import concourse.bass as bass
from concourse import mybir

ALU = mybir.AluOpType
ACT = mybir.ActivationFunctionType
F32 = mybir.dt.float32
F32R = mybir.dt.float32r

P = 128
D_MODEL = 1024
SEQ = 512
CHUNK = 64
EPS = 1e-6
A_HEADS, A_DIM = 8, 64
IDX_HEADS, IDX_DIM = 16, 64
B_HEADS, B_DIM = 4, 128
CONV_WIDTH = 4
TOPK = min(256, SEQ // 4)
ROPE_THETA = 500000.0
ROT = A_DIM // 4
HALF = ROT // 2
WIDTH = 512
TILES = SEQ // P
KT = D_MODEL // P
KW = WIDTH // P

SIZES = (("aq", 512), ("ak", 512), ("av", 512), ("az", 512), ("iq", 1024), ("ik", 64), ("iw", 16),
         ("bq", 512), ("bk", 512), ("bv", 512), ("bz", 512), ("bo", 512), ("bi", 4), ("bf", 4),
         ("ga", 1024), ("gb", 1024))
COL = {}
N_IN = 0
for _name, _size in SIZES:
    COL[_name] = N_IN
    N_IN += _size
SMALL_A = IDX_DIM + IDX_HEADS
SMALL = SMALL_A + 2 * B_HEADS

GROUPS = ("iq0", "iq1", "aq", "ak", "bq", "bk", "bv", "av", "bo", "bz", "az")
GROUP_COL = {"iq0": COL["iq"], "iq1": COL["iq"] + WIDTH, **{n: COL[n] for n in GROUPS[2:]}}
CHAN_GROUPS = ("bq", "bk")
UNITS = [("small", 0)] + [(g, j) for g in GROUPS for j in ((3, 2, 1) if g in ("iq0", "iq1") else range(TILES))]
UNIT = {u: n for n, u in enumerate(UNITS)}
N_IQ = 6
STAGED = [u for u in UNITS if u[0] in ("iq0", "iq1", "aq", "ak")]

SLOT = 1024
N_SMALL_SLOTS = 1
GATE0 = N_SMALL_SLOTS + 4 * len(GROUPS)
OUT0 = GATE0 + 3 * KT
N_SLOTS = OUT0 + KT
RAW = 3
SPLIT = 8
RELUS = 4


def group_slot(g):
    return N_SMALL_SLOTS + 4 * GROUPS.index(g)


SCORES = [(i, h) for i in (3, 2, 1) for h in range(IDX_HEADS)]
ATTN = [(i, h) for i in range(TILES) for h in range(A_HEADS)]


def first_quarter(g):
    return 4 * [u[0] for u in UNITS].index(g)


def score_place(s):
    return first_quarter("iq1") + 4 + (4 * s) // 5


def plan():
    at = {}

    def put(p, *job):
        at.setdefault(p, []).append(job)

    first = {g: first_quarter(g) for g in GROUPS}
    put(first["iq0"], "small_tok")
    put(first["iq0"] + 3, "ik_chan")
    put(first["iq0"] + 7, "gate_rows", 0)
    put(first["iq0"] + 7, "gate_rows", 1)
    put(first["iq1"] + 3, "gate_cols")
    for n, u in enumerate(STAGED):
        put(4 * UNIT[u] + 4 + 2, "stage_chan", n)
    for s in range(len(SCORES)):
        put(score_place(s), "score", s)
    for h in range(B_HEADS):
        p = first["av"] + 4 * h
        put(p, "decay_rows", h)
        put(p, "qk_b", h, 0)
        put(p + 1, "qk_b", h, 1)
        put(p + 2, "qk_b", h, 2)
        put(p + 3, "qk_b", h, 3)
        for i in range(TILES):
            put(p + 4 + i, "pv_b", h, i)
    for p in range(len(ATTN) + 4):
        q = first["bo"] + p
        if p >= 4:
            put(q, "pv_a", p - 4)
        if 2 <= p < len(ATTN) + 2:
            put(q, "probs_chan", p - 2)
        if p < len(ATTN):
            put(q, "qk_a", p)
    for j in range(TILES):
        put(first["bz"] + 4 * j + 7, "out_b_chan", j)
        if j < TILES - 1:
            put(first["az"] + 4 * j + 6, "out_a_chan", j)
    return at, first


SIDE, FIRST = plan()
LAST_SIDE = ("out_a_chan", TILES - 1)

RING_OF = {"small_tok": "tr", "ik_chan": "tr", "gate_rows": "tr", "gate_cols": "tr", "stage_chan": "tr",
           "decay_rows": "tr", "probs_chan": "tr", "out_a_chan": "tr", "out_b_chan": "tr",
           "score": "q", "qk_b": "q", "qk_a": "q", "pv_b": "o", "pv_a": "o"}


def fills():
    n = {"tr": 0, "q": 0, "o": 0}
    last = {}
    bank, before, order = {}, {}, {}
    for job in [job for p in sorted(SIDE) for job in SIDE[p]] + [LAST_SIDE]:
        order[job] = len(order)
        ring = RING_OF[job[0]]
        if job[0] == "pv_a" and ATTN[job[1]][1]:
            bank[job] = bank[("pv_a", job[1] - 1)]
            before[job] = None
        else:
            bank[job] = n[ring] % 2
            before[job] = last.get((ring, bank[job]))
            n[ring] += 1
        last[(ring, bank[job])] = job
    return bank, before, order


BANK, BEFORE, ORDER = fills()
OUT_ORDER = sorted([("out_a_chan", j) for j in range(TILES)] + [("out_b_chan", j) for j in range(TILES)],
                   key=ORDER.get)

ROUNDS = TOPK // 8


def round_plan():
    at = {}
    start = score_place(IDX_HEADS - 1) + 1
    for r in range(ROUNDS):
        at.setdefault(start + 2 * r, []).append((3, r))
    pairs = start + 2 * ROUNDS
    assert pairs > score_place(len(SCORES) - 1)
    for r in range(ROUNDS):
        at.setdefault(pairs + 3 * r, []).append((2, r))
        at.setdefault(pairs + 3 * r, []).append((1, r))
    return at


TOPK_AT = round_plan()
NO_KEY = -3.0e38
TAKEN = -3.3e38
BETWEEN = -3.15e38
MASKED = -1.0e30


def hybrid_kernel(nc, x, norm_g, w_in, conv_w, conv_b, b_igate, b_fgate, head_norm_g,
                  w_branch_a, w_branch_b, w_out, final_norm_g, ident_d, rope_d, out):
    ctx = ExitStack()
    with ctx:
        def sem(name):
            return ctx.enter_context(nc.semaphore(name))

        top = [(nc.sbuf_base + 31) // 32 * 32]

        def zone(size):
            at = top[0]
            top[0] += size
            return at

        def at(name, shape, dt, offset):
            return nc.alloc_sbuf_tensor_at(name, shape, dt, offset=offset)

        z_hhi, z_hlo = zone(16384), zone(16384)
        z_raw = zone(RAW * 4096)
        z_whi, z_wlo = zone(SPLIT * 4096), zone(SPLIT * 4096)
        z_const = zone(4096)
        z_negm = zone(2048)
        z_a = zone(18432)
        z_b = zone(6144)
        z_c = zone(16384)
        z_d = zone(8192)
        z_h = zone(12288)
        z_f = zone(16384)
        z_g1 = zone(8256)
        z_g2 = zone(8256)

        h_hi = at("h_hi", [P, KT, SEQ], F32R, z_hhi)
        h_lo = at("h_lo", [P, KT, SEQ], F32R, z_hlo)
        w_raw = at("w_raw", [P, RAW, SLOT], F32, z_raw)
        w_hi = at("w_hi", [P, SPLIT, SLOT], F32R, z_whi)
        w_lo = at("w_lo", [P, SPLIT, SLOT], F32R, z_wlo)

        o = [z_const]

        def const(name, shape):
            size = 4
            for n in shape[1:]:
                size *= n
            t = at(name, shape, F32, o[0])
            o[0] += (size + 31) // 32 * 32
            assert o[0] <= z_const + 4096
            return t

        ident = const("ident", [P, P])
        rope = const("rope", [P, TILES, 2, ROT])
        norm_col = const("norm_col", [P, KT])
        conv_w_col = const("conv_w_col", [P, 2 * B_HEADS, CONV_WIDTH])
        conv_b_col = const("conv_b_col", [P, 2 * B_HEADS])
        gate_bias = const("gate_bias", [P, 2 * B_HEADS])
        sumsq = const("sumsq", [P, TILES])
        rstd = const("rstd", [P, TILES])
        idx_w = const("idx_w", [P, TILES, IDX_HEADS])
        gate_x = const("gate_x", [P, TILES, 2 * B_HEADS])
        gate_t = const("gate_t", [P, TILES, B_HEADS])
        gate_l = const("gate_l", [P, TILES, 2 * B_HEADS])
        one_col = const("one_col", [P, 1])
        eps_col = const("eps_col", [P, 2])
        gate_tok = const("gate_tok", [P, 2, TILES, B_HEADS])
        en_m = const("en_m", [P, TILES, B_HEADS])
        top8 = const("top8", [P, TILES, 8])
        neg_max = const("neg_max", [P, len(ATTN)])
        p_sum = const("p_sum", [P, len(ATTN)])
        p_rec = const("p_rec", [P, len(ATTN)])
        den = const("den", [P, TILES, B_HEADS])
        bn6 = const("bn6", [P, B_HEADS, 6])
        mean_var = const("mean_var", [P, TILES, B_HEADS, 2])
        b_rstd = const("b_rstd", [P, TILES, B_HEADS])
        out_sq = const("out_sq", [P, TILES, 2])
        out_ms = const("out_ms", [P, TILES])
        out_rstd = const("out_rstd", [P, TILES])

        neg_m = at("neg_m", [B_HEADS, SEQ], F32, z_negm)
        relu = at("relu", [P, RELUS, WIDTH], F32, z_a)
        ik_hi = at("ik_hi", [P, SEQ], F32R, z_a + 10240)
        ik_lo = at("ik_lo", [P, SEQ], F32R, z_a + 12288)
        PACKED = P * TILES * (TILES + 1) // 2
        sp = at("sp", [P, 2, PACKED], F32, z_a)
        decay = at("decay", [P, 2, SEQ], F32, z_a + 10240)
        norm_b_row = at("norm_b_row", [P, WIDTH], F32, z_a + 14336)
        oa_hi = at("oa_hi", [P, KW, SEQ], F32R, z_a)
        oa_lo = at("oa_lo", [P, KW, SEQ], F32R, z_a + 8192)
        gate_ring = [at("gate_ring0", [P, WIDTH], F32, z_a + 16384), at("gate_ring1", [P, WIDTH], F32, z_negm)]
        score = at("score", [P, 3, WIDTH], F32, z_b)
        final_row = at("final_row", [P, D_MODEL], F32, z_b)
        mask0 = score[:, 0, 2 * P:3 * P]
        x_tok = at("x_tok", [P, TILES, D_MODEL], F32, z_c)
        small_chan = at("small_chan", [SMALL, SEQ], F32, z_c)
        small_tok = at("small_tok", [P, TILES, SMALL], F32, z_c + 2048)
        ik_twice = at("ik_twice", [P, TILES, P], F32, z_c + 4096)
        f_row = at("f_row", [B_HEADS, SEQ], F32, z_c + 6144)
        a_row = at("a_row", [B_HEADS, SEQ], F32, z_c + 8192)
        nm_row = at("nm_row", [B_HEADS, SEQ], F32, z_c + 10240)
        small_t = at("small_t", [P, TILES, ROT], F32, z_c + 12288)
        q_a = at("q_a", [P, KW, SEQ], F32, z_c)
        k_a = at("k_a", [P, KW, SEQ], F32, z_c + 8192)
        m_hi = at("m_hi", [P, KT, SEQ], F32R, z_c)
        m_lo = at("m_lo", [P, KT, SEQ], F32R, z_d)
        v_a = at("v_a", [P, TILES, WIDTH], F32, z_d)
        stage = at("stage", [P, 2, WIDTH], F32, z_h)
        rot_t = at("rot_t", [P, 2, A_HEADS, ROT], F32, z_h + 4096)
        U_LEN = SEQ + CONV_WIDTH
        conv_in = at("conv_in", [P, 2, U_LEN], F32, z_h + 6144)
        conv_acc = at("conv_acc", [P, 2, SEQ], F32, z_h)
        probs = at("probs", [P, 2, SEQ], F32, z_h)
        probs_t = at("probs_t", [P, 2, SEQ], F32, z_h + 4096)
        gated = at("gated", [P, 2, WIDTH], F32, z_h + 8192)
        x_norm = at("x_norm", [P, TILES, D_MODEL], F32, z_f)
        iq_parts = at("iq_parts", [P, 2, IDX_HEADS // 2, 3 * P], F32R, z_f)
        assert z_g1 == z_f + 16384
        qk_b = at("qk_b", [P, 2 * B_HEADS, SEQ], F32, z_f)
        ob_hi = at("ob_hi", [P, KW, SEQ], F32R, z_f)
        ob_lo = at("ob_lo", [P, KW, SEQ], F32R, z_f + 8192)
        v_b = at("v_b", [P, TILES, B_HEADS, B_DIM + 1], F32, z_g1)
        o_a = at("o_a", [P, TILES, WIDTH], F32, z_g1)
        cell = at("cell", [P, TILES, B_HEADS, B_DIM + 1], F32, z_g2)
        sig = at("sig", [P, 2, 2, WIDTH], F32, z_g1)
        prod = at("prod", [P, 2, 2, WIDTH], F32, z_g2)
        x_again = at("x_again", [P, TILES, D_MODEL], F32, z_hhi)
        y_tok = at("y_tok", [P, 2, D_MODEL], F32, z_hlo)
        y_norm = at("y_norm", [P, 2, D_MODEL], F32, z_hlo + 8192)
        square = at("square", [P, 2, WIDTH], F32, z_g1)

        pj = [ctx.enter_context(nc.psum_tensor(f"pj{b}", [P, WIDTH], F32)) for b in range(2)]
        tr = [ctx.enter_context(nc.psum_tensor(f"tr{b}", [P, WIDTH], F32)) for b in range(2)]
        qb = [ctx.enter_context(nc.psum_tensor(f"qb{b}", [P, WIDTH], F32)) for b in range(2)]
        ob = [ctx.enter_context(nc.psum_tensor(f"ob{b}", [P, WIDTH], F32)) for b in range(2)]
        start_banks = [pj[0], pj[1], tr[0], tr[1], qb[0], qb[1], ob[0], ob[1]]
        BANKS = {"tr": tr, "q": qb, "o": ob}

        x_in = [sem(f"x_in{j}") for j in range(TILES)]
        const_in = sem("const_in")
        late_in = sem("late_in")
        norm_row_in = sem("norm_row_in")
        final_row_in = sem("final_row_in")
        x_again_in = sem("x_again_in")
        raw_in = [sem(f"raw_in{r}") for r in range(RAW)]
        hi_made = sem("hi_made")
        lo_made = sem("lo_made")
        slot_used = sem("slot_used")
        x_squared = sem("x_squared")
        x_root = sem("x_root")
        x_scaled = sem("x_scaled")
        x_turned = sem("x_turned")
        h_hi_made = sem("h_hi_made")
        h_lo_made = sem("h_lo_made")
        unit_full = sem("unit_full")
        unit_out = sem("unit_out")
        side_done = sem("side_done")
        small_copied = sem("small_copied")
        ik_ready = sem("ik_ready")
        ik_hi_made = sem("ik_hi_made")
        ik_lo_made = sem("ik_lo_made")
        iq_hi_made = sem("iq_hi_made")
        v_ones_made = sem("v_ones_made")
        rows_read = sem("rows_read")
        gate_in = sem("gate_in")
        gate_ln = sem("gate_ln")
        gate_logs = sem("gate_logs")
        rows_ready = sem("rows_ready")
        gate_tok_made = sem("gate_tok_made")
        en_made = sem("en_made")
        rotated = sem("rotated")
        iq_turned = sem("iq_turned")
        qk_a_turned = sem("qk_a_turned")
        relu_made = sem("relu_made")
        relu_used = sem("relu_used")
        conv_done = sem("conv_done")
        qk_b_ready = sem("qk_b_ready")
        decay_made = sem("decay_made")
        decay_cut = sem("decay_cut")
        sp_made = sem("sp_made")
        cell_made = sem("cell_made")
        gate_t_made = sem("gate_t_made")
        bo_scaled = sem("bo_scaled")
        zt_made = sem("zt_made")
        z_made = sem("z_made")
        probs_made = sem("probs_made")
        probs_t_made = sem("probs_t_made")
        o_a_made = sem("o_a_made")
        b_var_made = sem("b_var_made")
        b_root = sem("b_root")
        zg_scaled = sem("zg_scaled")
        gated_made = sem("gated_made")
        o_hi = sem("o_hi")
        o_lo = sem("o_lo")
        pad_made = sem("pad_made")
        eps_made = sem("eps_made")
        sig_made = sem("sig_made")
        sig_used = sem("sig_used")
        branch_full = sem("branch_full")
        branch_free = sem("branch_free")
        merged = sem("merged")
        m_hi_made = sem("m_hi_made")
        m_lo_made = sem("m_lo_made")
        last_m_lo_made = sem("last_m_lo_made")
        y_added = sem("y_added")
        y_squared = sem("y_squared")
        y_ms = sem("y_ms")
        y_root = sem("y_root")
        y_made = sem("y_made")
        stored = [sem(f"stored{b}") for b in range(2)]
        dve_step = sem("dve_step")
        act_step = sem("act_step")
        pool_step = sem("pool_step")

        block = ctx.enter_context(nc.Block())

        def slot_pos(n):
            if n < GATE0:
                return n % SPLIT
            if n < OUT0:
                return (GATE0 + 3 * ((n - GATE0) // 3 % 2) + (n - GATE0) % 3) % SPLIT
            return (n - OUT0 + GATE0 + 6) % SPLIT

        def slot_before(n):
            for m in range(n - 1, -1, -1):
                if slot_pos(m) == slot_pos(n):
                    return m
            return None

        def bank_of(job):
            return BANKS[RING_OF[job[0]]][BANK[job]]

        def wait_full(eng, job):
            eng.wait_ge(side_done, ORDER[job] + 1)

        def wait_read(eng, job):
            kind = job[0]
            if kind == "small_tok":
                eng.wait_ge(small_copied, 1)
            elif kind == "ik_chan":
                eng.wait_ge(ik_lo_made, 1)
            elif kind == "gate_rows":
                eng.wait_ge(rows_read, 2 - job[1])
            elif kind == "gate_cols":
                eng.wait_ge(gate_tok_made, 1)
            elif kind == "stage_chan":
                if job[1] < N_IQ:
                    eng.wait_ge(iq_turned, 2 * job[1] + 2)
                else:
                    eng.wait_ge(qk_a_turned, job[1] - N_IQ + 1)
            elif kind == "score":
                eng.wait_ge(relu_made, job[1] + 1)
            elif kind == "decay_rows":
                eng.wait_ge(decay_cut, (job[1] + 1) * TILES)
            elif kind == "qk_b":
                eng.wait_ge(sp_made, job[1] * TILES + job[2] + 1)
            elif kind == "pv_b":
                eng.wait_ge(cell_made, job[1] * TILES + job[2] + 1)
            elif kind == "qk_a":
                eng.wait_ge(z_made, job[1] + 1)
            elif kind == "probs_chan":
                eng.wait_ge(probs_t_made, job[1] + 1)
            elif kind == "pv_a":
                eng.wait_ge(o_a_made, ATTN[job[1]][0] + 1)
            else:
                eng.wait_ge(o_lo, OUT_ORDER.index(job) + 1)

        def wait_unit_read(eng, u):
            if u >= len(UNITS) + 2 * KT:
                eng.wait_ge(y_added, u - len(UNITS) - 2 * KT + 1)
            elif u >= len(UNITS):
                eng.wait_ge(sig_made, u - len(UNITS) + 1)
            elif UNITS[u][0] == "bo":
                eng.wait_ge(gate_t_made, UNITS[u][1] + 1)
            elif UNITS[u][0] in ("bz", "az"):
                eng.wait_ge(zt_made, u - UNIT[("bz", 0)] + 1)
            else:
                eng.wait_ge(unit_out, u + 1)

        def wait_slot_used(eng, n):
            if n < N_SMALL_SLOTS:
                eng.wait_ge(unit_full, 1)
            elif n < GATE0:
                g, q = divmod(n - N_SMALL_SLOTS, 4)
                if q < 3:
                    eng.wait_ge(slot_used, 3 * g + q + 1)
                else:
                    eng.wait_ge(unit_full, max(u for u, v in enumerate(UNITS) if v[0] == GROUPS[g]) + 1)
            elif n < OUT0:
                c, q = divmod(n - GATE0, 3)
                if q < 2:
                    eng.wait_ge(unit_full, len(UNITS) + 2 * c + q + 1)
                else:
                    eng.wait_ge(branch_full, 2 * c + 2)

        def iq_part(job, e):
            g, j = STAGED[job[1]]
            b0 = 0 if g == "iq0" else 4
            same, other = slice(e * IDX_DIM, (e + 1) * IDX_DIM), slice((1 - e) * IDX_DIM, (2 - e) * IDX_DIM)
            cols = slice((j - 1) * P, j * P)
            return (bank_of(job)[same, :].rearrange("p (b t) -> p b t", t=P),
                    iq_parts[same, e, b0:b0 + 4, cols], iq_parts[other, e, b0:b0 + 4, cols])

        def unit_slots(u):
            g, j = UNITS[u]
            if g == "small":
                return []
            n = group_slot(g) + 4
            if g in ("iq0", "iq1"):
                return {3: [n, n + 1], 2: [n + 2], 1: [n + 3]}[j]
            if g == "az":
                return [n + j] if j < 3 else []
            return [n + j]

        @block.sync
        def _(sp):
            w_in_k = w_in.rearrange("(k p) n -> p k n", p=P)
            wa_k = w_branch_a.rearrange("(k p) n -> p k n", p=P)
            wb_k = w_branch_b.rearrange("(k p) n -> p k n", p=P)
            x_t = x.rearrange("(t p) d -> p t d", p=P)
            for j in range(TILES):
                sp.dma_start(x_tok[:, j, :], x_t[:, j, :]).then_inc(x_in[j], 16)

            def load(n):
                r = n % RAW
                if n >= RAW:
                    sp.wait_ge(lo_made, n - RAW + 1)
                raw = w_raw[:, r, :]
                if n == 0:
                    small = raw[:, 0:KT * SMALL].rearrange("p (k n) -> p k n", n=SMALL)
                    sp.dma_start(small[:, :, 0:SMALL_A], w_in_k[:, :, COL["ik"]:COL["ik"] + SMALL_A])\
                        .then_inc(raw_in[r], 16)
                    sp.dma_start(small[:, :, SMALL_A:SMALL], w_in_k[:, :, COL["bi"]:COL["bi"] + 2 * B_HEADS])\
                        .then_inc(raw_in[r], 16)
                elif n < GATE0:
                    g, q = divmod(n - N_SMALL_SLOTS, 4)
                    c = GROUP_COL[GROUPS[g]]
                    sp.dma_start(raw.rearrange("p (k n) -> p k n", n=WIDTH),
                                 w_in_k[:, 2 * q:2 * q + 2, c:c + WIDTH]).then_inc(raw_in[r], 16)
                elif n < OUT0:
                    c, q = divmod(n - GATE0, 3)
                    dst = raw.rearrange("p (k n) -> p k n", n=P)
                    if q < 2:
                        col = COL["ga" if q == 0 else "gb"] + c * P
                        sp.dma_start(dst, w_in_k[:, :, col:col + P]).then_inc(raw_in[r], 16)
                    else:
                        sp.dma_start(dst[:, 0:KW, :], wa_k[:, :, c * P:(c + 1) * P]).then_inc(raw_in[r], 16)
                        sp.dma_start(dst[:, KW:2 * KW, :], wb_k[:, :, c * P:(c + 1) * P]).then_inc(raw_in[r], 16)
                else:
                    k = n - OUT0
                    sp.dma_start(raw, w_out[k * P:(k + 1) * P, :]).then_inc(raw_in[r], 16)

            for n in range(N_SLOTS):
                load(n)
                if n == RAW - 1:
                    sp.dma_start(rope[:, :, :, :], rope_d.rearrange("(t p) a d -> p t a d", p=P)).then_inc(late_in, 16)
                    sp.dma_start(gate_bias[:, 0:B_HEADS], b_igate.partition_broadcast(P)).then_inc(late_in, 16)
                    sp.dma_start(gate_bias[:, B_HEADS:2 * B_HEADS], b_fgate.partition_broadcast(P)).then_inc(late_in, 16)
                    sp.dma_start(conv_b_col[:, :], conv_b).then_inc(late_in, 16)
                    sp.dma_start(conv_w_col[:, :, :], conv_w).then_inc(late_in, 16)
                if n == group_slot("bo"):
                    sp.wait_ge(relu_used, len(SCORES))
                    sp.dma_start(norm_b_row[:, :], head_norm_g.partition_broadcast(P)).then_inc(norm_row_in, 16)
                if n == GATE0 + 6:
                    sp.wait_ge(z_made, len(ATTN))
                    sp.dma_start(final_row[:, :], final_norm_g.partition_broadcast(P)).then_inc(final_row_in, 16)
            wait_slot_used(sp, OUT0 - 2)
            sp.dma_start(x_again[:, :, :], x_t).then_inc(x_again_in, 16)
            out_t = out.rearrange("(t p) d -> p t d", p=P)
            for i in range(TILES):
                sp.wait_ge(y_made, i + 1)
                sp.dma_start(out_t[:, i, :], y_norm[:, i % 2, :]).then_inc(stored[i % 2], 16)
            for b in range(2):
                sp.wait_ge(stored[b], 16 * TILES // 2)

        def raw_count(n):
            def dmas(m):
                return 2 if m == 0 or (GATE0 <= m < OUT0 and (m - GATE0) % 3 == 2) else 1
            return 16 * sum(dmas(m) for m in range(n % RAW, n + 1, RAW))

        def slot_size(n):
            return KT * SMALL if n == 0 else SLOT

        @block.gpsimd
        def _(pool):
            pool.memset(one_col[:, :], 1.0)
            pool.memset(eps_col[:, 0:1], EPS)
            pool.memset(eps_col[:, 1:2], 4 * EPS).then_inc(eps_made, 1)
            pool.memset(mask0, 0.0).then_inc(pool_step, 1)
            pool.wait_ge(pool_step, 1)
            pool.memset(mask0[0:CHUNK, CHUNK:P], MASKED)
            pool.memset(conv_in[:, :, 0:CONV_WIDTH], 0.0).then_inc(pad_made, 1)

            def remainder(n):
                pool.wait_ge(hi_made, n + 1)
                m, p = slot_size(n), slot_pos(n)
                pool.tensor_tensor(w_lo[:, p, 0:m], w_raw[:, n % RAW, 0:m], w_hi[:, p, 0:m].bitcast(F32),
                                   ALU.subtract).then_inc(lo_made, 1)

            def side(p):
                for job in SIDE.get(p, []):
                    if job[0] == "qk_b":
                        h, j = job[1:]
                        e = h * TILES + j
                        pool.wait_ge(decay_made, e + 1)
                        d = decay[:, e % 2, 0:P]
                        pool.affine_select(out=d, in_=d, compare_op=ALU.is_ge, fill=0.0, base=0,
                                           pattern=[[1, P]], channel_multiplier=-1).then_inc(decay_cut, 1)

            for n in range(N_SMALL_SLOTS + 4):
                remainder(n)
            for u, (g, j) in enumerate(UNITS):
                for n in unit_slots(u):
                    remainder(n)
                for q in range(4):
                    side(4 * u + q)
                if (g, j) == ("bq", 0):
                    wait_full(pool, ("score", len(SCORES) - 1))
                    pool.memset(v_b[:, :, :, B_DIM:B_DIM + 1], 1.0).then_inc(v_ones_made, 1)
                if g == "bz":
                    if j == 0:
                        pool.wait_ge(norm_row_in, 16)
                    pool.wait_ge(zt_made, j + 1)
                    pool.tensor_tensor(gated[:, j % 2, :], gated[:, j % 2, :], norm_b_row[:, :], ALU.mult)\
                        .then_inc(zg_scaled, 1)
            for c in range(KT):
                for n in range(GATE0 + 3 * (c + 1), GATE0 + 3 * (c + 2)):
                    remainder(n)
                if c == KT - 1:
                    break
                pool.wait_ge(m_hi_made, c + 1)
                pool.tensor_tensor(m_lo[:, c, :], prod[:, c % 2, 0, :], m_hi[:, c, :].bitcast(F32), ALU.subtract)\
                    .then_inc(m_lo_made, 1)
            for n in range(OUT0 + 3, N_SLOTS):
                remainder(n)

        @block.scalar
        def _(act):
            steps = [0]

            def link(ins):
                steps[0] += 1
                ins.then_inc(act_step, 1)
                act.wait_ge(act_step, steps[0])

            act.dma_start(ident[:, :], ident_d).then_inc(const_in, 16)
            act.dma_start(norm_col[:, :], norm_g).then_inc(const_in, 16)
            act.wait_ge(eps_made, 1)
            link(act.activation(rstd[:, 0:1], eps_col[:, 0:1], ACT.Sqrt))

            for j in range(TILES):
                act.wait_ge(x_in[j], 16)
                act.activation(x_norm[:, j, :], x_tok[:, j, :], ACT.Square, accum_out=sumsq[:, j:j + 1])\
                    .then_inc(x_squared, 1)
                act.wait_ge(x_squared, j + 1)
                act.activation(rstd[:, j:j + 1], sumsq[:, j:j + 1], ACT.Sqrt, bias=eps_col[:, 0:1],
                               scale=1.0 / D_MODEL).then_inc(x_root, 1)

            def round_slot(n):
                act.wait_ge(raw_in[n % RAW], raw_count(n))
                if slot_before(n) is not None:
                    wait_slot_used(act, slot_before(n))
                m = slot_size(n)
                act.activation(w_hi[:, slot_pos(n), 0:m], w_raw[:, n % RAW, 0:m], ACT.Copy).then_inc(hi_made, 1)

            round_slot(0)
            act.wait_ge(const_in, 32)
            for k in range(KT):
                act.wait_ge(x_turned, k + 1)
                act.activation(h_hi[:, k, :], start_banks[k][:, :], ACT.Copy, scale=norm_col[:, k:k + 1])\
                    .then_inc(h_hi_made, 1)
                if k in (1, 4, 7):
                    round_slot(1 + k // 3)
            round_slot(4)

            def job_side(job):
                kind = job[0]
                if kind == "ik_chan":
                    wait_full(act, job)
                    act.activation(ik_hi[:, :], bank_of(job)[:, :], ACT.Copy).then_inc(ik_hi_made, 1)
                elif kind == "small_tok":
                    act.wait_ge(gate_in, 1)
                    link(act.activation(gate_t[:, :, :], gate_t[:, :, :], ACT.Exp, scale=-1.0))
                    act.activation(gate_t[:, :, :], gate_t[:, :, :], ACT.Ln, bias=one_col[:, 0:1])\
                        .then_inc(gate_ln, 1)
                elif kind == "gate_cols":
                    act.wait_ge(gate_tok_made, 1)
                    act.activation(en_m[:, :, :], gate_tok[:, 1, :, :], ACT.Exp).then_inc(en_made, 1)
                elif kind == "stage_chan" and STAGED[job[1]][0] in ("iq0", "iq1"):
                    wait_full(act, job)
                    for e in range(2):
                        src, hi, _ = iq_part(job, e)
                        act.activation(hi, src, ACT.Copy).then_inc(iq_hi_made, 1)
                elif kind == "stage_chan":
                    g, j = STAGED[job[1]]
                    dst = q_a if g == "aq" else k_a
                    if g == "aq" and j == 0:
                        act.wait_ge(gate_tok_made, 1)
                    wait_full(act, job)
                    act.activation(dst[:, :, j * P:(j + 1) * P],
                                   bank_of(job)[:, :].rearrange("p (b t) -> p b t", t=P), ACT.Copy)\
                        .then_inc(qk_a_turned, 1)
                elif kind == "score":
                    s = job[1]
                    i, h = SCORES[s]
                    w = (i + 1) * P
                    wait_full(act, job)
                    if s >= RELUS:
                        act.wait_ge(relu_used, s - RELUS + 1)
                    act.activation(relu[:, s % RELUS, 0:w], bank_of(job)[:, 0:w], ACT.Relu,
                                   scale=float(IDX_DIM) ** -0.5).then_inc(relu_made, 1)
                elif kind == "qk_b":
                    h, j = job[1:]
                    e = h * TILES + j
                    rows = ("decay_rows", h)
                    if j == 0:
                        wait_full(act, rows)
                    if e >= 2:
                        act.wait_ge(sp_made, e - 1)
                    act.activation(decay[:, e % 2, 0:SEQ - j * P], bank_of(rows)[:, j * P:SEQ], ACT.Exp,
                                   bias=gate_tok[:, 0, j, h:h + 1]).then_inc(decay_made, 1)
                elif kind == "pv_b":
                    h, i = job[1:]
                    wait_full(act, job)
                    act.activation(cell[:, i, h, :], bank_of(job)[:, 0:B_DIM + 1], ACT.Copy)\
                        .then_inc(cell_made, 1)
                elif kind == "qk_a":
                    s = job[1]
                    w = (ATTN[s][0] + 1) * P
                    act.wait_ge(z_made, s + 1)
                    act.activation(probs[:, s % 2, 0:w], probs[:, s % 2, 0:w], ACT.Exp, scale=-1.0,
                                   bias=neg_max[:, s:s + 1], accum_out=p_sum[:, s:s + 1])\
                        .then_inc(probs_made, 1)
                elif kind in ("out_a_chan", "out_b_chan"):
                    j = job[1]
                    dst = oa_hi if kind == "out_a_chan" else ob_hi
                    wait_full(act, job)
                    act.activation(dst[:, :, j * P:(j + 1) * P],
                                   bank_of(job)[:, :].rearrange("p (b t) -> p b t", t=P), ACT.Copy, scale=0.5)\
                        .then_inc(o_hi, 1)

            def evacuate(u):
                g, j = UNITS[u]
                src = pj[u % 2]
                done = unit_out
                act.wait_ge(unit_full, u + 1)
                if g == "small":
                    act.activation(small_chan[:, :], src[0:SMALL, :], ACT.Copy).then_inc(done, 1)
                elif g in ("iq0", "iq1", "aq", "ak"):
                    n = STAGED.index((g, j))
                    if n >= 2:
                        old = ("stage_chan", n - 2)
                        wait_full(act, old)
                    act.activation(stage[:, n % 2, :], src[:, :], ACT.Copy).then_inc(done, 1)
                elif g in CHAN_GROUPS:
                    b = j + (0 if g == "bq" else B_HEADS)
                    if b == 0:
                        wait_full(act, ("stage_chan", len(STAGED) - 1))
                        act.wait_ge(late_in, 16 * 5)
                    if b >= 2:
                        act.wait_ge(conv_done, b - 1)
                    act.activation(conv_in[:, b % 2, CONV_WIDTH:], src[:, :], ACT.Copy)
                    if b >= 2:
                        act.wait_ge(qk_b_ready, b - 1)
                    act.activation(conv_acc[:, b % 2, :], src[:, :], ACT.Identity,
                                   scale=conv_w_col[:, b, CONV_WIDTH - 1:CONV_WIDTH],
                                   bias=conv_b_col[:, b:b + 1]).then_inc(done, 1)
                elif g == "bv":
                    act.activation(v_b[:, j, :, 0:B_DIM], src[:, :].rearrange("p (h d) -> p h d", d=B_DIM), ACT.Copy)\
                        .then_inc(done, 1)
                elif g == "av":
                    act.activation(v_a[:, j, :], src[:, :], ACT.Copy).then_inc(done, 1)
                else:
                    n = 4 * ("bo", "bz", "az").index(g) + j
                    if 2 <= n < 2 + TILES:
                        act.wait_ge(bo_scaled, n - 1)
                    elif n >= 2 + TILES:
                        act.wait_ge(zt_made, n - 1 - TILES)
                    act.activation(gate_ring[n % 2][:, :], src[:, :], ACT.Tanh, scale=0.5).then_inc(gate_t_made, 1)

            def silu_conv(b):
                act.wait_ge(conv_done, b + 1)
                act.activation(qk_b[:, b, :], conv_acc[:, b % 2, :], ACT.Silu).then_inc(qk_b_ready, 1)

            for u, (g, j) in enumerate(UNITS):
                for n in unit_slots(u):
                    round_slot(n)
                for q in range(4):
                    if q == 3:
                        evacuate(u)
                    for job in SIDE.get(4 * u + q, []):
                        job_side(job)
                    if q == 3 and UNITS[u - 1][0] in CHAN_GROUPS:
                        b = UNITS[u - 1][1] + (0 if UNITS[u - 1][0] == "bq" else B_HEADS)
                        silu_conv(b)
                if (g, j) == ("bz", 0):
                    act.wait_ge(b_var_made, TILES)
                    act.activation(b_rstd[:, :, :], mean_var[:, :, :, 1], ACT.Sqrt, bias=eps_col[:, 1:2])\
                        .then_inc(b_root, 1)

            for c in range(KT):
                for n in range(GATE0 + 3 * (c + 1), GATE0 + 3 * (c + 2)):
                    round_slot(n)
                for s in range(2):
                    if c == KT - 1:
                        round_slot(OUT0 + 3 + 2 * s)
                    u = len(UNITS) + 2 * c + s
                    act.wait_ge(unit_full, u + 1)
                    if c >= 2:
                        act.wait_ge(sig_used, 2 * (c - 2) + s + 1)
                    if c == 0 and s == 0:
                        act.wait_ge(gated_made, 2 * TILES)
                    act.activation(sig[:, c % 2, s, :], pj[u % 2][:, :], ACT.Sigmoid).then_inc(sig_made, 1)
                    if c == 0 and s == 0:
                        job_side(LAST_SIDE)
                    if c == KT - 1:
                        round_slot(OUT0 + 4 + 2 * s)
                if c == KT - 1:
                    round_slot(OUT0 + 7)
                act.wait_ge(merged, c + 1)
                act.activation(m_hi[:, c, :], prod[:, c % 2, 0, :], ACT.Copy).then_inc(m_hi_made, 1)
            for i in range(TILES):
                for s in range(2):
                    n = 2 * i + s
                    act.wait_ge(y_added, n + 1)
                    if n >= 2:
                        act.wait_ge(y_squared, n - 1)
                    act.activation(square[:, n % 2, :], y_tok[:, i % 2, s * WIDTH:(s + 1) * WIDTH], ACT.Square,
                                   accum_out=out_sq[:, i, s:s + 1]).then_inc(y_squared, 1)
                act.wait_ge(y_ms, i + 1)
                act.activation(out_rstd[:, i:i + 1], out_ms[:, i:i + 1], ACT.Sqrt, bias=eps_col[:, 0:1],
                               scale=1.0 / D_MODEL).then_inc(y_root, 1)

        @block.vector
        def _(dve):
            steps = [0]

            def link(ins):
                steps[0] += 1
                ins.then_inc(dve_step, 1)
                dve.wait_ge(dve_step, steps[0])

            for j in range(TILES):
                dve.wait_ge(x_root, j + 1)
                link(dve.reciprocal(rstd[:, j:j + 1], rstd[:, j:j + 1]))
                dve.tensor_scalar(x_norm[:, j, :], x_tok[:, j, :], rstd[:, j:j + 1], None, ALU.mult)\
                    .then_inc(x_scaled, 1)
            dve.wait_ge(const_in, 32)
            for k in range(KT):
                dve.wait_ge(h_hi_made, k + 1)
                dve.scalar_tensor_tensor(out=h_lo[:, k, :], in0=start_banks[k][:, :], scalar=norm_col[:, k:k + 1],
                                         in1=h_hi[:, k, :].bitcast(F32), op0=ALU.mult, op1=ALU.subtract)\
                    .then_inc(h_lo_made, 1)
            dve.wait_ge(late_in, 16 * 5)

            def rotate(dst, src, tmp, cos, sin):
                link(dve.tensor_tensor(tmp[..., 0:HALF], src[..., HALF:ROT], sin[..., 0:HALF], ALU.mult))
                link(dve.tensor_tensor(tmp[..., HALF:ROT], src[..., 0:HALF], sin[..., HALF:ROT], ALU.mult))
                link(dve.tensor_tensor(dst[..., 0:ROT], src[..., 0:ROT], cos, ALU.mult))
                return dve.tensor_tensor(dst[..., 0:ROT], dst[..., 0:ROT], tmp, ALU.add)

            def absolute(dst, src):
                return dve.scalar_tensor_tensor(out=dst, in0=src, scalar=-1.0, in1=src, op0=ALU.mult, op1=ALU.max)

            def small(job):
                wait_full(dve, job)
                dve.tensor_copy(small_tok[:, :, :],
                                bank_of(job)[:, 0:TILES * SMALL].rearrange("p (t n) -> p t n", n=SMALL))\
                    .then_inc(small_copied, 1)
                dve.wait_ge(small_copied, 1)
                link(dve.tensor_tensor(gate_x[:, :, :], small_tok[:, :, SMALL_A:SMALL],
                                       gate_bias[:, :].unsqueeze(1).to_broadcast([P, TILES, 2 * B_HEADS]), ALU.add))
                absolute(gate_t[:, :, :], gate_x[:, :, B_HEADS:2 * B_HEADS]).then_inc(gate_in, 1)
                link(rotate(small_tok[:, :, 0:ROT], small_tok[:, :, 0:ROT], small_t[:, :, :],
                            rope[:, :, 0, :], rope[:, :, 1, :]))
                link(dve.tensor_copy(ik_twice[:, :, 0:IDX_DIM], small_tok[:, :, 0:IDX_DIM]))
                dve.tensor_copy(ik_twice[:, :, IDX_DIM:P], small_tok[:, :, 0:IDX_DIM]).then_inc(ik_ready, 1)
                dve.tensor_scalar(idx_w[:, :, :], small_tok[:, :, IDX_DIM:SMALL_A], float(IDX_HEADS) ** -0.5,
                                  None, ALU.mult)
                link(dve.tensor_copy(gate_l[:, :, 0:B_HEADS], gate_x[:, :, 0:B_HEADS]))
                link(dve.tensor_scalar(gate_l[:, :, B_HEADS:], gate_x[:, :, B_HEADS:], 0.0, None, ALU.min))
                dve.wait_ge(gate_ln, 1)
                dve.tensor_tensor(gate_l[:, :, B_HEADS:], gate_l[:, :, B_HEADS:], gate_t[:, :, :], ALU.subtract)\
                    .then_inc(gate_logs, 1)

            def rows(job):
                if job[1] == 0:
                    return
                li, lf = ("gate_rows", 0), ("gate_rows", 1)
                wait_full(dve, lf)
                ones = one_col[0:B_HEADS, 0:1].to_broadcast([B_HEADS, SEQ])
                dve.tensor_tensor_scan(f_row[:, :], ones, bank_of(lf)[0:B_HEADS, :], 0.0, ALU.mult, ALU.add)\
                    .then_inc(rows_read, 1)
                dve.wait_ge(rows_read, 1)
                dve.tensor_tensor(a_row[:, :], bank_of(li)[0:B_HEADS, :], f_row[:, :], ALU.subtract)\
                    .then_inc(rows_read, 1)
                dve.wait_ge(rows_read, 2)
                link(dve.tensor_tensor_scan(nm_row[:, :], a_row[:, :], a_row[:, :], 0.0, ALU.max, ALU.max))
                link(dve.tensor_scalar(neg_m[:, :], nm_row[:, :], -1.0, None, ALU.mult))
                dve.tensor_tensor(nm_row[:, :], neg_m[:, :], f_row[:, :], ALU.subtract).then_inc(rows_ready, 1)

            def score_step(job):
                s = job[1]
                i, h = SCORES[s]
                w = (i + 1) * P
                acc = score[:, i - 1, 0:w]
                dve.wait_ge(relu_made, s + 1)
                wt = idx_w[:, i, h:h + 1]
                if h == 0:
                    ins = dve.tensor_scalar(acc, relu[:, s % RELUS, 0:w], wt, None, ALU.mult)
                else:
                    dve.wait_ge(relu_used, s)
                    ins = dve.scalar_tensor_tensor(out=acc, in0=relu[:, s % RELUS, 0:w], scalar=wt, in1=acc,
                                                   op0=ALU.mult, op1=ALU.add)
                ins.then_inc(relu_used, 1)
                if h == IDX_HEADS - 1:
                    dve.wait_ge(relu_used, s + 1)
                    link(dve.memset(score[0:CHUNK, i - 1, w - CHUNK:w], NO_KEY))

            def top_round(i, r):
                w = (i + 1) * P
                acc = score[:, i - 1, 0:w]
                link(dve.max(top8[:, i, :], acc))
                link(dve.match_replace(acc, top8[:, i, :], acc, TAKEN))
                if r == ROUNDS - 1:
                    link(dve.tensor_scalar(acc, acc, BETWEEN, MASKED, ALU.is_gt, ALU.mult))

            def conv(b):
                if b == 0:
                    dve.wait_ge(pad_made, 1)
                wait_unit_read(dve, UNIT[("bq", 0)] + b)
                for t in range(CONV_WIDTH - 1):
                    ins = dve.scalar_tensor_tensor(
                        out=conv_acc[:, b % 2, :], in0=conv_in[:, b % 2, t + 1:t + 1 + SEQ],
                        scalar=conv_w_col[:, b, t:t + 1], in1=conv_acc[:, b % 2, :], op0=ALU.mult, op1=ALU.add)
                    if t < CONV_WIDTH - 2:
                        link(ins)
                ins.then_inc(conv_done, 1)

            def packed(j):
                return P * (TILES * j - j * (j - 1) // 2)

            def job_side(job):
                kind = job[0]
                if kind == "small_tok":
                    small(job)
                elif kind == "gate_rows":
                    rows(job)
                elif kind == "gate_cols":
                    wait_full(dve, job)
                    dve.tensor_copy(gate_tok[:, :, :, :].rearrange("p a t h -> p (a t h)"),
                                    bank_of(job)[:, 0:2 * TILES * B_HEADS]).then_inc(gate_tok_made, 1)
                elif kind == "ik_chan":
                    dve.wait_ge(ik_hi_made, 1)
                    dve.tensor_tensor(ik_lo[:, :], bank_of(job)[:, :], ik_hi[:, :].bitcast(F32), ALU.subtract)\
                        .then_inc(ik_lo_made, 1)
                elif kind == "stage_chan" and STAGED[job[1]][0] in ("iq0", "iq1"):
                    for e in range(2):
                        src, hi, lo = iq_part(job, e)
                        dve.wait_ge(iq_hi_made, 2 * job[1] + e + 1)
                        dve.tensor_tensor(lo, src, hi.bitcast(F32), ALU.subtract).then_inc(iq_turned, 1)
                elif kind == "score":
                    score_step(job)
                elif kind == "qk_b":
                    h, j = job[1:]
                    e = h * TILES + j
                    w = SEQ - j * P
                    wait_full(dve, job)
                    dve.wait_ge(decay_cut, e + 1)
                    if h >= 2 and j == 0:
                        wait_full(dve, ("pv_b", h - 2, TILES - 1))
                    dve.scalar_tensor_tensor(out=sp[:, h % 2, packed(j):packed(j) + w], in0=bank_of(job)[:, 0:w],
                                             scalar=float(B_DIM) ** -0.5, in1=decay[:, e % 2, 0:w],
                                             op0=ALU.mult, op1=ALU.mult).then_inc(sp_made, 1)
                elif kind == "qk_a":
                    s = job[1]
                    i, h = ATTN[s]
                    w = (i + 1) * P
                    mask = mask0 if i == 0 else score[:, i - 1, 0:w]
                    wait_full(dve, job)
                    if s >= 2:
                        wait_full(dve, ("probs_chan", s - 2))
                    dve.tensor_tensor_reduce(out=probs[:, s % 2, 0:w], in0=bank_of(job)[:, 0:w], in1=mask,
                                             scale=-float(A_DIM) ** -0.5, scalar=3.0e38, op0=ALU.add, op1=ALU.min,
                                             accum_out=neg_max[:, s:s + 1]).then_inc(z_made, 1)
                elif kind == "probs_chan":
                    s = job[1]
                    w = (ATTN[s][0] + 1) * P
                    wait_full(dve, job)
                    if s >= 2:
                        wait_full(dve, ("pv_a", s - 2))
                    dve.tensor_copy(probs_t[:, s % 2, 0:w], bank_of(job)[:, 0:w]).then_inc(probs_t_made, 1)
                elif kind == "pv_a":
                    s = job[1]
                    i, h = ATTN[s]
                    if h == A_HEADS - 1:
                        wait_full(dve, job)
                        dve.wait_ge(probs_made, s + 1)
                        rec = p_rec[:, s - h:s + 1]
                        link(dve.reciprocal(rec, p_sum[:, s - h:s + 1]))
                        dve.tensor_tensor(o_a[:, i, :].rearrange("p (h d) -> p h d", d=A_DIM),
                                          bank_of(job)[:, :].rearrange("p (h d) -> p h d", d=A_DIM),
                                          rec.unsqueeze(2).to_broadcast([P, A_HEADS, A_DIM]), ALU.mult)\
                            .then_inc(o_a_made, 1)
                elif kind in ("out_a_chan", "out_b_chan"):
                    j = job[1]
                    n = OUT_ORDER.index(job)
                    hi, lo = (oa_hi, oa_lo) if kind == "out_a_chan" else (ob_hi, ob_lo)
                    dve.wait_ge(o_hi, n + 1)
                    dve.scalar_tensor_tensor(
                        out=lo[:, :, j * P:(j + 1) * P], in0=bank_of(job)[:, :].rearrange("p (b t) -> p b t", t=P),
                        scalar=0.5, in1=hi[:, :, j * P:(j + 1) * P].bitcast(F32), op0=ALU.mult, op1=ALU.subtract)\
                        .then_inc(o_lo, 1)

            def cell_scale():
                wait_read(dve, ("pv_b", B_HEADS - 1, TILES - 1))
                dve.wait_ge(en_made, 1)
                link(absolute(den[:, :, :], cell[:, :, :, B_DIM]))
                link(dve.tensor_tensor(den[:, :, :], den[:, :, :], en_m[:, :, :], ALU.max))
                link(dve.reciprocal(den[:, :, :], den[:, :, :]))

            def unit(u):
                g, j = UNITS[u]
                if g in ("iq0", "iq1", "aq", "ak"):
                    n = STAGED.index((g, j))
                    wait_unit_read(dve, u)
                    st = stage[:, n % 2, :].rearrange("p (h d) -> p h d", d=A_DIM)
                    cos = rope[:, j, 0, :].unsqueeze(1).to_broadcast([P, A_HEADS, ROT])
                    sin = rope[:, j, 1, :].unsqueeze(1).to_broadcast([P, A_HEADS, ROT])
                    rotate(st, st, rot_t[:, n % 2, :, :], cos, sin).then_inc(rotated, 1)
                elif g in CHAN_GROUPS:
                    conv(j + (0 if g == "bq" else B_HEADS))
                elif g == "bo":
                    if j == 0:
                        cell_scale()
                    dve.wait_ge(gate_t_made, j + 1)
                    c = cell[:, j, :, 0:B_DIM]
                    link(dve.tensor_tensor(c, c, den[:, j, :].unsqueeze(2).to_broadcast([P, B_HEADS, B_DIM]), ALU.mult))
                    ins = dve.scalar_tensor_tensor(out=c, in0=gate_ring[j % 2][:, :].rearrange("p (h d) -> p h d", d=B_DIM),
                                                   scalar=1.0, in1=c, op0=ALU.add, op1=ALU.mult)
                    ins.then_inc(bo_scaled, 1)
                    dve.wait_ge(bo_scaled, j + 1)
                    for h in range(B_HEADS):
                        ins = dve.bn_stats(bn6[:, h, :], cell[:, j, h, 0:B_DIM])
                    link(ins)
                    for h in range(B_HEADS):
                        ins = dve.bn_aggr(mean_var[:, j, h, :], bn6[:, h, :])
                    ins.then_inc(b_var_made, 1)
                    dve.wait_ge(b_var_made, j + 1)
                elif g in ("bz", "az"):
                    n = 4 * ("bo", "bz", "az").index(g) + j
                    m = n - 4
                    dve.wait_ge(gate_t_made, n + 1)
                    if m >= 2:
                        wait_full(dve, OUT_ORDER[m - 2])
                    ring = gated[:, m % 2, :]
                    ins = dve.scalar_tensor_tensor(out=ring, in0=gate_ring[n % 2][:, :], scalar=1.0,
                                                   in1=pj[u % 2][:, :], op0=ALU.add, op1=ALU.mult)
                    ins.then_inc(zt_made, 1)
                    dve.wait_ge(zt_made, m + 1)
                    if g == "az":
                        dve.tensor_tensor(ring, ring, o_a[:, j, :], ALU.mult).then_inc(gated_made, 1)
                    else:
                        if j == 0:
                            dve.wait_ge(b_root, 1)
                            link(dve.reciprocal(b_rstd[:, :, :], b_rstd[:, :, :]))
                        for h in range(B_HEADS):
                            c = cell[:, j, h, 0:B_DIM]
                            ins = dve.tensor_scalar(c, c, mean_var[:, j, h, 0:1], b_rstd[:, j, h:h + 1],
                                                    ALU.subtract, ALU.mult)
                        link(ins)
                        dve.wait_ge(zg_scaled, j + 1)
                        dve.tensor_tensor(ring.rearrange("p (h d) -> p h d", d=B_DIM),
                                          ring.rearrange("p (h d) -> p h d", d=B_DIM), cell[:, j, :, 0:B_DIM],
                                          ALU.mult).then_inc(gated_made, 1)

            for u in range(len(UNITS)):
                for q in range(4):
                    p = 4 * u + q
                    for job in SIDE.get(p, []):
                        job_side(job)
                    for i, r in TOPK_AT.get(p, []):
                        top_round(i, r)
                unit(u)

            for c in range(KT):
                if c == 0:
                    job_side(LAST_SIDE)
                for s in range(2):
                    n = 2 * c + s
                    u = len(UNITS) + n
                    wait_unit_read(dve, u)
                    dve.wait_ge(branch_full, n + 1)
                    if c >= 2:
                        dve.wait_ge(m_lo_made, c - 1)
                    bank = (qb if s == 0 else ob)[c % 2]
                    dve.tensor_tensor(prod[:, c % 2, s, :], bank[:, :], sig[:, c % 2, s, :], ALU.mult)\
                        .then_inc(sig_used, 1)
                dve.wait_ge(sig_used, 2 * c + 2)
                dve.tensor_tensor(prod[:, c % 2, 0, :], prod[:, c % 2, 0, :], prod[:, c % 2, 1, :], ALU.add)\
                    .then_inc(merged, 1)
            dve.wait_ge(m_hi_made, KT)
            dve.wait_ge(merged, KT)
            dve.tensor_tensor(m_lo[:, KT - 1, :], prod[:, (KT - 1) % 2, 0, :], m_hi[:, KT - 1, :].bitcast(F32),
                              ALU.subtract).then_inc(last_m_lo_made, 1)

            dve.wait_ge(x_again_in, 16)
            dve.wait_ge(final_row_in, 16)
            for i in range(TILES):
                for s in range(2):
                    n = 2 * i + s
                    u = len(UNITS) + 2 * KT + n
                    dve.wait_ge(unit_full, u + 1)
                    cols = slice(s * WIDTH, (s + 1) * WIDTH)
                    if i >= 2:
                        dve.wait_ge(y_made, i - 1)
                    dve.tensor_tensor(y_tok[:, i % 2, cols], pj[u % 2][:, :], x_again[:, i, cols], ALU.add)\
                        .then_inc(y_added, 1)
                dve.wait_ge(y_squared, 2 * i + 2)
                dve.tensor_tensor(out_ms[:, i:i + 1], out_sq[:, i, 0:1], out_sq[:, i, 1:2], ALU.add).then_inc(y_ms, 1)
                dve.wait_ge(y_root, i + 1)
                link(dve.reciprocal(out_rstd[:, i:i + 1], out_rstd[:, i:i + 1]))
                if i >= 2:
                    dve.wait_ge(stored[i % 2], 16)
                dve.scalar_tensor_tensor(out=y_norm[:, i % 2, :], in0=y_tok[:, i % 2, :], scalar=out_rstd[:, i:i + 1],
                                         in1=final_row[:, :], op0=ALU.mult, op1=ALU.mult).then_inc(y_made, 1)

        @block.tensor
        def _(pe):
            def three(bank, a, b, first, last):
                (a_hi, a_lo), (b_hi, b_lo) = a, b
                pe.matmul(bank, a_hi, b_hi, start=first, stop=False)
                pe.matmul(bank, a_hi, b_lo, start=False, stop=False)
                return pe.matmul(bank, a_lo, b_hi, start=False, stop=last)

            def w_part(n, a, b):
                p = slot_pos(n)
                return w_hi[:, p, a:b], w_lo[:, p, a:b]

            def h_part(k, a, b):
                return h_hi[:, k, a:b], h_lo[:, k, a:b]

            pe.wait_ge(const_in, 32)
            for j in range(TILES):
                pe.wait_ge(x_scaled, j + 1)
                for k in range(KT):
                    ins = pe.transpose(start_banks[k][:, j * P:(j + 1) * P], x_norm[:, j, k * P:(k + 1) * P], ident[:, :])
                    if j == TILES - 1:
                        ins.then_inc(x_turned, 1)

            def side(job):
                kind = job[0]
                bank = bank_of(job)
                if BEFORE[job] is not None:
                    wait_read(pe, BEFORE[job])
                if kind == "small_tok":
                    wait_unit_read(pe, 0)
                    for j in range(TILES):
                        ins = pe.transpose(bank[:, j * SMALL:(j + 1) * SMALL], small_chan[:, j * P:(j + 1) * P],
                                           ident[0:SMALL, 0:SMALL])
                elif kind == "ik_chan":
                    pe.wait_ge(ik_ready, 1)
                    for j in range(TILES):
                        ins = pe.transpose(bank[:, j * P:(j + 1) * P], ik_twice[:, j, :], ident[:, :])
                elif kind == "gate_rows":
                    pe.wait_ge(gate_logs, 1)
                    c = job[1] * B_HEADS
                    for j in range(TILES):
                        ins = pe.transpose(bank[0:B_HEADS, j * P:(j + 1) * P], gate_l[:, j, c:c + B_HEADS], ident[:, :])
                elif kind == "gate_cols":
                    pe.wait_ge(rows_ready, 1)
                    for a, row in enumerate((a_row, nm_row)):
                        for j in range(TILES):
                            c = (a * TILES + j) * B_HEADS
                            ins = pe.transpose(bank[:, c:c + B_HEADS], row[:, j * P:(j + 1) * P],
                                               ident[0:B_HEADS, 0:B_HEADS])
                elif kind == "stage_chan":
                    n = job[1]
                    pe.wait_ge(rotated, n + 1)
                    for b in range(4):
                        ins = pe.transpose(bank[:, b * P:(b + 1) * P], stage[:, n % 2, b * P:(b + 1) * P], ident[:, :])
                elif kind == "score":
                    s = job[1]
                    i, h = SCORES[s]
                    w = (i + 1) * P
                    if s == 0:
                        wait_read(pe, ("ik_chan",))
                    if s in (0, 8, 24, 40):
                        wait_read(pe, ("stage_chan", STAGED.index(("iq0" if h < 8 else "iq1", i))))
                    queries = iq_parts[:, h % 2, h // 2, (i - 1) * P:i * P]
                    pe.matmul(bank[:, 0:w], queries, ik_hi[:, 0:w], start=True, stop=False)
                    ins = pe.matmul(bank[:, 0:w], queries, ik_lo[:, 0:w], start=False, stop=True)
                elif kind == "decay_rows":
                    h = job[1]
                    ins = pe.matmul(bank[:, :], ident[0:B_HEADS, h:h + 1].to_broadcast([B_HEADS, P]), neg_m[:, :],
                                    start=True, stop=True)
                elif kind == "qk_b":
                    h, j = job[1:]
                    if j == 0:
                        pe.wait_ge(qk_b_ready, 2 * B_HEADS if h == 0 else 1)
                    ins = pe.matmul(bank[:, 0:SEQ - j * P], qk_b[:, B_HEADS + h, j * P:(j + 1) * P],
                                    qk_b[:, h, j * P:SEQ], start=True, stop=True)
                elif kind == "pv_b":
                    h, i = job[1:]
                    wait_read(pe, ("qk_b", h, i))
                    if h == 0 and i == 0:
                        pe.wait_ge(v_ones_made, 1)
                    for j in range(i + 1):
                        c = P * (TILES * j - j * (j - 1) // 2) + (i - j) * P
                        ins = pe.matmul(bank[:, 0:B_DIM + 1], sp[:, h % 2, c:c + P], v_b[:, j, h, :],
                                        start=(j == 0), stop=(j == i))
                elif kind == "qk_a":
                    s = job[1]
                    i, h = ATTN[s]
                    w = (i + 1) * P
                    if s == 0:
                        wait_read(pe, ("stage_chan", len(STAGED) - 1))
                    r = slice((h % 2) * A_DIM, (h % 2 + 1) * A_DIM)
                    ins = pe.matmul(bank[:, 0:w], q_a[r, h // 2, i * P:(i + 1) * P], k_a[r, h // 2, 0:w],
                                    start=True, stop=True)
                elif kind == "probs_chan":
                    s = job[1]
                    pe.wait_ge(probs_made, s + 1)
                    for j in range(ATTN[s][0] + 1):
                        ins = pe.transpose(bank[:, j * P:(j + 1) * P], probs[:, s % 2, j * P:(j + 1) * P], ident[:, :])
                elif kind == "pv_a":
                    s = job[1]
                    i, h = ATTN[s]
                    wait_read(pe, ("probs_chan", s))
                    for j in range(i + 1):
                        ins = pe.matmul(bank[:, h * A_DIM:(h + 1) * A_DIM], probs_t[:, s % 2, j * P:(j + 1) * P],
                                        v_a[:, j, h * A_DIM:(h + 1) * A_DIM], start=(j == 0), stop=(j == i))
                elif kind in ("out_a_chan", "out_b_chan"):
                    pe.wait_ge(gated_made, OUT_ORDER.index(job) + 1)
                    ring = gated[:, OUT_ORDER.index(job) % 2, :]
                    for b in range(KW):
                        ins = pe.transpose(bank[:, b * P:(b + 1) * P], ring[:, b * P:(b + 1) * P], ident[:, :])
                ins.then_inc(side_done, 1)

            for u, (g, j) in enumerate(UNITS):
                bank = pj[u % 2]
                if u >= 2:
                    wait_unit_read(pe, u - 2)
                if g == "small":
                    pe.wait_ge(lo_made, 1)
                    for k in range(KT):
                        pe.wait_ge(h_lo_made, k + 1)
                        ins = three(bank[0:SMALL, :], w_part(0, k * SMALL, (k + 1) * SMALL), h_part(k, 0, SEQ),
                                    k == 0, k == KT - 1)
                    ins.then_inc(unit_full, 1)
                    continue
                units = [v for v in UNITS if v[0] == g]
                for q in range(4):
                    n = group_slot(g) + q
                    if (g, j) == units[0]:
                        pe.wait_ge(lo_made, n + 1)
                    for k in (2 * q, 2 * q + 1):
                        c = (k % 2) * WIDTH
                        if g in CHAN_GROUPS:
                            a, b = w_part(n, c + j * P, c + (j + 1) * P), h_part(k, 0, SEQ)
                        else:
                            a, b = h_part(k, j * P, (j + 1) * P), w_part(n, c, c + WIDTH)
                        ins = three(bank[:, :], a, b, k == 0, k == KT - 1)
                    if q == 3:
                        ins.then_inc(unit_full, 1)
                    elif (g, j) == units[-1]:
                        ins.then_inc(slot_used, 1)
                    for job in SIDE.get(4 * u + q, []):
                        side(job)

            for c in range(KT):
                for s in range(2):
                    u = len(UNITS) + 2 * c + s
                    n = GATE0 + 3 * c + s
                    wait_unit_read(pe, u - 2)
                    pe.wait_ge(lo_made, n + 1)
                    for k in range(KT):
                        ins = three(pj[u % 2][:, :], w_part(n, k * P, (k + 1) * P), h_part(k, 0, SEQ), k == 0, k == KT - 1)
                    ins.then_inc(unit_full, 1)
                    if c == 0 and s == 0:
                        side(LAST_SIDE)
                n = GATE0 + 3 * c + 2
                pe.wait_ge(lo_made, n + 1)
                if c == 0:
                    pe.wait_ge(o_lo, 2 * TILES)
                for s, (hi, lo) in enumerate(((ob_hi, ob_lo), (oa_hi, oa_lo))[::-1]):
                    if c >= 2:
                        pe.wait_ge(sig_used, 2 * (c - 2) + s + 1)
                    bank = (qb if s == 0 else ob)[c % 2]
                    for k in range(KW):
                        ins = three(bank[:, :], w_part(n, (s * KW + k) * P, (s * KW + k + 1) * P),
                                    (hi[:, k, :], lo[:, k, :]), k == 0, k == KW - 1)
                    ins.then_inc(branch_full, 1)

            for i in range(TILES):
                for s in range(2):
                    u = len(UNITS) + 2 * KT + 2 * i + s
                    wait_unit_read(pe, u - 2)
                    for k in range(KT):
                        if i == 0 and s == 0:
                            if k < KT - 1:
                                pe.wait_ge(m_lo_made, k + 1)
                            else:
                                pe.wait_ge(last_m_lo_made, 1)
                            pe.wait_ge(lo_made, OUT0 + k + 1)
                        t = slice(i * P, (i + 1) * P)
                        ins = three(pj[u % 2][:, :], (m_hi[:, k, t], m_lo[:, k, t]),
                                    w_part(OUT0 + k, s * WIDTH, (s + 1) * WIDTH), k == 0, k == KT - 1)
                    ins.then_inc(unit_full, 1)


_INS = ["x", "norm_g", "w_in", "conv_w", "conv_b", "b_igate", "b_fgate", "head_norm_g",
        "w_branch_a", "w_branch_b", "w_out", "final_norm_g"]


def _rope_table():
    import numpy as np

    inv = np.float32(ROPE_THETA) ** (-(np.arange(HALF, dtype=np.float32) * np.float32(2.0) / np.float32(ROT)))
    ang = np.arange(SEQ, dtype=np.float32)[:, None] * inv.astype(np.float32)[None, :]
    cos, sin = np.cos(ang), np.sin(ang)
    return np.stack([np.concatenate([cos, cos], 1), np.concatenate([-sin, sin], 1)], 1).astype(np.float32)


def kernel(**inputs):
    import numpy as np
    import concourse.bacc as bacc
    from concourse.bass_utils import run_bass_kernel_spmd

    nc = bacc.Bacc("TRN2", target_bir_lowering=False, num_devices=1)
    arrays, args = {}, []

    def give(name, a):
        arrays[name] = a
        args.append(nc.dram_tensor(name, a.shape, mybir.dt.from_np(a.dtype), kind="ExternalInput").ap())

    for name in _INS:
        a = np.asarray(inputs[name])
        if name != "final_norm_g":
            a = a[0]
        if name in ("norm_g", "conv_b"):
            a = a.reshape(-1, P).T
        if name == "conv_w":
            a = a.reshape(CONV_WIDTH, -1, P).transpose(2, 1, 0)
        give(f"in_{name}", np.ascontiguousarray(a))
    give("const_ident", np.eye(P, dtype=np.float32))
    give("const_rope", _rope_table())
    args.append(nc.dram_tensor("out_0", (SEQ, D_MODEL), F32, kind="ExternalOutput").ap())
    hybrid_kernel(nc, *args)
    r = run_bass_kernel_spmd(nc, [arrays], core_ids=[0])
    return r.results[0]["out_0"].reshape(1, SEQ, D_MODEL)
```

```python
from contextlib import ExitStack

import concourse.bass as bass
from concourse import mybir

ALU = mybir.AluOpType
ACT = mybir.ActivationFunctionType
F32 = mybir.dt.float32
F32R = mybir.dt.float32r

P = 128
D_MODEL = 1024
SEQ = 512
CHUNK = 64
EPS = 1e-6
A_HEADS, A_DIM = 8, 64
IDX_HEADS, IDX_DIM = 16, 64
B_HEADS, B_DIM = 4, 128
CONV_WIDTH = 4
TOPK = min(256, SEQ // 4)
ROPE_THETA = 500000.0
ROT = A_DIM // 4
HALF = ROT // 2
WIDTH = 512
TILES = SEQ // P
KT = D_MODEL // P
KW = WIDTH // P

SIZES = (("aq", 512), ("ak", 512), ("av", 512), ("az", 512), ("iq", 1024), ("ik", 64), ("iw", 16),
         ("bq", 512), ("bk", 512), ("bv", 512), ("bz", 512), ("bo", 512), ("bi", 4), ("bf", 4),
         ("ga", 1024), ("gb", 1024))
COL = {}
N_IN = 0
for _name, _size in SIZES:
    COL[_name] = N_IN
    N_IN += _size
SMALL_A = IDX_DIM + IDX_HEADS
SMALL = SMALL_A + 2 * B_HEADS

GROUPS = ("iq0", "iq1", "aq", "ak", "bq", "bk", "bv", "av", "bo", "bz", "az")
GROUP_COL = {"iq0": COL["iq"], "iq1": COL["iq"] + WIDTH, **{n: COL[n] for n in GROUPS[2:]}}
CHAN_GROUPS = ("bq", "bk")
UNITS = [("small", 0)] + [(g, j) for g in GROUPS for j in ((3, 2, 1) if g in ("iq0", "iq1") else range(TILES))]
UNIT = {u: n for n, u in enumerate(UNITS)}
N_IQ = 6
STAGED = [u for u in UNITS if u[0] in ("iq0", "iq1", "aq", "ak")]

SLOT = 1024
N_SMALL_SLOTS = 1
GATE0 = N_SMALL_SLOTS + 4 * len(GROUPS)
OUT0 = GATE0 + 3 * KT
N_SLOTS = OUT0 + KT
DVE_SLOTS = (0, OUT0 + 2, OUT0 + 4, OUT0 + 6, OUT0 + 7)
RAW = 3
LAST_PLACE = OUT0 + KT - 2
LATE0 = OUT0 + KT - 3
SPLIT = 7
RELUS = 4


def group_slot(g):
    return N_SMALL_SLOTS + 4 * GROUPS.index(g)


SCORES = [(i, h) for i in (3, 2, 1) for h in range(IDX_HEADS)]
ATTN = [(i, h) for i in range(TILES) for h in range(A_HEADS)]


def first_quarter(g):
    return 4 * [u[0] for u in UNITS].index(g)


def score_place(s):
    return first_quarter("iq1") + 4 + (4 * s) // 5


def attn_place(s):
    return first_quarter("bo") + 7 + s


SPLIT_AT = {attn_place(A_HEADS * i - 6) if i else attn_place(-3): i for i in range(TILES)}


def plan():
    at = {}

    def put(p, *job):
        at.setdefault(p, []).append(job)

    first = {g: first_quarter(g) for g in GROUPS}
    put(first["iq0"], "small_tok")
    put(first["iq0"] + 3, "ik_chan")
    put(first["iq0"] + 8, "gate_rows", 1)
    put(first["iq0"] + 8, "gate_rows", 0)
    put(first["iq1"] + 3, "gate_cols")
    for n, u in enumerate(STAGED):
        put(4 * UNIT[u] + 4 + 2, "stage_chan", n)
    for s in range(len(SCORES)):
        put(score_place(s), "score", s)
    for h in range(B_HEADS):
        p = first["av"] + 4 * h
        put(p, "decay_rows", h)
        put(p, "qk_b", h, 0)
        put(p + 1, "qk_b", h, 1)
        put(p + 2, "qk_b", h, 2)
        put(p + 3, "qk_b", h, 3)
        for i in range(TILES):
            put(p + 4 + i, "pv_b", h, i)
    for p in range(len(ATTN) + 4):
        q = attn_place(p)
        if p >= 4:
            put(q, "pv_a", p - 4)
        if 2 <= p < len(ATTN) + 2:
            put(q, "probs_chan", p - 2)
        if p < len(ATTN):
            put(q, "qk_a", p)
    for j in range(TILES):
        put(first["bz"] + 4 * j + 7, "out_b_chan", j)
        if j < TILES - 1:
            put(first["az"] + 4 * j + 6, "out_a_chan", j)
    return at, first


SIDE, FIRST = plan()
OUT_UNITS = [(i, s, slice(s * WIDTH, (s + 1) * WIDTH)) for i in range(TILES) for s in range(2)][:-1] + \
    [(TILES - 1, 1, slice(WIDTH, WIDTH + WIDTH // 2)), (TILES - 1, 2, slice(WIDTH + WIDTH // 2, 2 * WIDTH))]
LAST_SIDE = ("out_a_chan", TILES - 1)

RING_OF = {"small_tok": "tr", "ik_chan": "tr", "gate_rows": "tr", "gate_cols": "tr", "stage_chan": "tr",
           "decay_rows": "tr", "probs_chan": "tr", "out_a_chan": "tr", "out_b_chan": "tr",
           "score": "q", "qk_b": "q", "qk_a": "q", "pv_b": "o", "pv_a": "o"}


def fills():
    n = {"tr": 0, "q": 0, "o": 0}
    last = {}
    bank, before, order = {}, {}, {}
    for job in [job for p in sorted(SIDE) for job in SIDE[p]] + [LAST_SIDE]:
        order[job] = len(order)
        ring = RING_OF[job[0]]
        if job[0] == "pv_a" and ATTN[job[1]][1]:
            bank[job] = bank[("pv_a", job[1] - 1)]
            before[job] = None
        else:
            bank[job] = n[ring] % 2
            before[job] = last.get((ring, bank[job]))
            n[ring] += 1
        last[(ring, bank[job])] = job
    return bank, before, order


BANK, BEFORE, ORDER = fills()
OUT_ORDER = sorted([("out_a_chan", j) for j in range(TILES)] + [("out_b_chan", j) for j in range(TILES)],
                   key=ORDER.get)

ROUNDS = TOPK // 8


def round_plan():
    at = {}
    start = score_place(IDX_HEADS - 1) + 1
    place = start
    for r in range(ROUNDS):
        at.setdefault(place, []).append((3, r))
        place += 4 if first_quarter("ak") <= place < first_quarter("bq") else 2
    pairs = place
    assert pairs > score_place(len(SCORES) - 1)
    for r in range(ROUNDS):
        at.setdefault(pairs + 3 * r, []).append((2, r))
        at.setdefault(pairs + 3 * r, []).append((1, r))
    return at


TOPK_AT = round_plan()
NO_KEY = -3.0e38
TAKEN = -3.3e38
BETWEEN = -3.15e38
MASKED = -1.0e30


def hybrid_kernel(nc, x, norm_g, w_in, conv_w, conv_b, b_igate, b_fgate, head_norm_g,
                  w_branch_a, w_branch_b, w_out, final_norm_g, ident_d, rope_d, out):
    ctx = ExitStack()
    with ctx:
        def sem(name):
            return ctx.enter_context(nc.semaphore(name))

        top = [(nc.sbuf_base + 31) // 32 * 32]

        def zone(size):
            at = top[0]
            top[0] += size
            return at

        def at(name, shape, dt, offset):
            return nc.alloc_sbuf_tensor_at(name, shape, dt, offset=offset)

        z_hhi, z_hlo = zone(16384), zone(16384)
        z_raw = zone(RAW * 4096)
        z_whi, z_wlo = zone(SPLIT * 4096), zone(SPLIT * 4096)
        z_const = zone(4096)
        z_negm = zone(2048)
        z_a = zone(18432)
        z_b = zone(6144)
        z_c = zone(16384)
        z_e = zone(8192)
        z_d = zone(8192)
        z_h = zone(12288)
        z_f = zone(16384)
        z_g1 = zone(8256)
        z_g2 = zone(8256)

        h_hi = at("h_hi", [P, KT, SEQ], F32R, z_hhi)
        h_lo = at("h_lo", [P, KT, SEQ], F32R, z_hlo)
        w_raw = at("w_raw", [P, RAW, SLOT], F32, z_raw)
        w_hi = at("w_hi", [P, SPLIT, SLOT], F32R, z_whi)
        w_lo = at("w_lo", [P, SPLIT, SLOT], F32R, z_wlo)

        o = [z_const]

        def const(name, shape, dt=F32):
            size = 4
            for n in shape[1:]:
                size *= n
            t = at(name, shape, dt, o[0])
            o[0] += (size + 31) // 32 * 32
            assert o[0] <= z_const + 4096
            return t

        ident = const("ident", [P, P])
        rope = const("rope", [P, TILES, 2, ROT])
        norm_col = const("norm_col", [P, KT])
        conv_w_col = const("conv_w_col", [P, 2 * B_HEADS, CONV_WIDTH])
        conv_b_col = const("conv_b_col", [P, 2 * B_HEADS])
        gate_bias = const("gate_bias", [P, 2 * B_HEADS])
        sumsq = const("sumsq", [P, TILES])
        rstd = const("rstd", [P, TILES])
        idx_w = const("idx_w", [P, TILES, IDX_HEADS])
        gate_x = const("gate_x", [P, TILES, 2 * B_HEADS])
        gate_t = const("gate_t", [P, TILES, B_HEADS])
        gate_l = const("gate_l", [P, TILES, 2 * B_HEADS])
        one_col = const("one_col", [P, 1])
        head_row = const("head_row", [B_HEADS, B_HEADS], F32R)
        eps_col = const("eps_col", [P, 2])
        gate_tok = const("gate_tok", [P, 2, TILES, B_HEADS])
        en_m = const("en_m", [P, TILES, B_HEADS])
        top8 = const("top8", [P, TILES, 8])
        neg_max = const("neg_max", [P, len(ATTN)])
        p_sum = const("p_sum", [P, len(ATTN)])
        p_rec = const("p_rec", [P, len(ATTN)])
        den = const("den", [P, TILES, B_HEADS])
        bn6 = const("bn6", [P, B_HEADS, 6])
        mean_var = const("mean_var", [P, TILES, B_HEADS, 2])
        b_rstd = const("b_rstd", [P, TILES, B_HEADS])
        out_sq = const("out_sq", [P, TILES, 3])
        out_ms = const("out_ms", [P, TILES])
        out_rstd = const("out_rstd", [P, TILES])

        neg_m_hi = at("neg_m_hi", [B_HEADS, SEQ], F32R, z_negm)
        neg_m_lo = at("neg_m_lo", [B_HEADS, SEQ], F32R, z_a + 16384)
        relu = at("relu", [P, RELUS, WIDTH], F32, z_a)
        ik_hi = at("ik_hi", [P, SEQ], F32R, z_a + 10240)
        ik_lo = at("ik_lo", [P, SEQ], F32R, z_a + 12288)
        PACKED = P * TILES * (TILES + 1) // 2
        sp = at("sp", [P, 2, PACKED], F32, z_a)
        decay = at("decay", [P, 2, SEQ], F32, z_a + 10240)
        norm_b_row = at("norm_b_row", [P, WIDTH], F32, z_a + 14336)
        oa_hi = at("oa_hi", [P, KW, SEQ], F32R, z_a)
        oa_lo = at("oa_lo", [P, KW, SEQ], F32R, z_a + 8192)
        gate_ring = [at("gate_ring0", [P, WIDTH], F32, z_a + 16384), at("gate_ring1", [P, WIDTH], F32, z_negm)]
        score = at("score", [P, 3, WIDTH], F32, z_b)
        mask0 = score[:, 0, 2 * P:3 * P]
        x_tok = at("x_tok", [P, TILES, D_MODEL], F32, z_c)
        small_chan = at("small_chan", [SMALL, SEQ], F32, z_c)
        small_tok = at("small_tok", [P, TILES, SMALL], F32, z_c + 2048)
        ik_twice = at("ik_twice", [P, TILES, P], F32, z_c + 4096)
        f_row = at("f_row", [B_HEADS, SEQ], F32, z_c + 6144)
        a_row = at("a_row", [B_HEADS, SEQ], F32, z_c + 8192)
        nm_row = at("nm_row", [B_HEADS, SEQ], F32, z_c + 10240)
        small_t = at("small_t", [P, TILES, ROT], F32, z_c + 12288)
        k_parts = at("k_parts", [P, 2, A_HEADS // 2, SEQ], F32R, z_c)
        m_hi = at("m_hi", [P, KT, SEQ], F32R, z_c)
        m_lo = at("m_lo", [P, KT, SEQ], F32R, z_d)
        q_a = at("q_a", [P, KW, SEQ], F32, z_e)
        q_twice = at("q_twice", [P, 2, 2, A_HEADS // 2, P], F32R, z_a)
        q_lo = at("q_lo", [P, 2, A_HEADS // 2, P], F32R, z_a + 8192)
        v_a = at("v_a", [P, TILES, WIDTH], F32, z_d)
        stage = at("stage", [P, 2, WIDTH], F32, z_h)
        rot_t = at("rot_t", [P, 2, A_HEADS, ROT], F32, z_h + 4096)
        U_LEN = SEQ + CONV_WIDTH
        conv_in = at("conv_in", [P, 2, U_LEN], F32, z_h + 6144)
        conv_acc = at("conv_acc", [P, 2, SEQ], F32, z_h)
        probs = at("probs", [P, 2, SEQ], F32, z_h)
        probs_t = at("probs_t", [P, 2, SEQ], F32, z_h + 4096)
        gated = at("gated", [P, 2, WIDTH], F32, z_h + 8192)
        assert z_b == z_a + 18432
        w_late = [at(f"w_late{n}", [P, SLOT], F32, place)
                  for n, place in enumerate((z_a + 16384, z_a + 20480, z_h + 8192))]
        x_norm = at("x_norm", [P, TILES, D_MODEL], F32, z_f)
        iq_parts = at("iq_parts", [P, 2, IDX_HEADS // 2, 3 * P], F32R, z_f)
        assert z_g1 == z_f + 16384
        qk_b = at("qk_b", [P, 2 * B_HEADS, SEQ], F32, z_f)
        ob_hi = at("ob_hi", [P, KW, SEQ], F32R, z_f)
        ob_lo = at("ob_lo", [P, KW, SEQ], F32R, z_f + 8192)
        v_b = at("v_b", [P, TILES, B_HEADS, B_DIM + 1], F32, z_g1)
        o_a = at("o_a", [P, TILES, WIDTH], F32, z_g1)
        cell = at("cell", [P, TILES, B_HEADS, B_DIM + 1], F32, z_g2)
        sig = at("sig", [P, 2, 2, WIDTH], F32, z_g1)
        prod = at("prod", [P, 2, 2, WIDTH], F32, z_g2)
        x_again = at("x_again", [P, TILES, D_MODEL], F32, z_hhi)
        final_row = at("final_row", [P, D_MODEL], F32, z_a + 8192)
        w_last = [at("w_last_hi", [P, SLOT], F32R, z_a), at("w_last_lo", [P, SLOT], F32R, z_a + 4096)]
        y_tok = at("y_tok", [P, 2, D_MODEL], F32, z_hlo)
        y_norm = at("y_norm", [P, 2, D_MODEL], F32, z_hlo + 8192)
        square = at("square", [P, 2, WIDTH], F32, z_g1)

        pj = [ctx.enter_context(nc.psum_tensor(f"pj{b}", [P, WIDTH], F32)) for b in range(2)]
        tr = [ctx.enter_context(nc.psum_tensor(f"tr{b}", [P, WIDTH], F32)) for b in range(2)]
        qb = [ctx.enter_context(nc.psum_tensor(f"qb{b}", [P, WIDTH], F32)) for b in range(2)]
        ob = [ctx.enter_context(nc.psum_tensor(f"ob{b}", [P, WIDTH], F32)) for b in range(2)]
        start_banks = [pj[0], pj[1], tr[0], tr[1], qb[0], qb[1], ob[0], ob[1]]
        BANKS = {"tr": tr, "q": qb, "o": ob}

        x_in = [sem(f"x_in{j}") for j in range(TILES)]
        const_in = sem("const_in")
        late_in = sem("late_in")
        norm_row_in = sem("norm_row_in")
        final_row_in = sem("final_row_in")
        x_again_in = sem("x_again_in")
        raw_in = [sem(f"raw_in{r}") for r in range(RAW + N_SLOTS - LATE0)]
        hi_made = sem("hi_made")
        lo_by_pool = sem("lo_by_pool")
        lo_by_dve = sem("lo_by_dve")
        slot_used = sem("slot_used")
        x_squared = sem("x_squared")
        x_root = sem("x_root")
        x_scaled = sem("x_scaled")
        x_turned = sem("x_turned")
        h_hi_made = sem("h_hi_made")
        h_lo_made = sem("h_lo_made")
        unit_full = sem("unit_full")
        unit_out = sem("unit_out")
        side_done = sem("side_done")
        small_copied = sem("small_copied")
        ik_ready = sem("ik_ready")
        ik_hi_made = sem("ik_hi_made")
        ik_lo_made = sem("ik_lo_made")
        v_ones_made = sem("v_ones_made")
        rows_read = sem("rows_read")
        gate_in = sem("gate_in")
        gate_ln = sem("gate_ln")
        gate_logs = sem("gate_logs")
        rows_ready = sem("rows_ready")
        gate_tok_made = sem("gate_tok_made")
        en_made = sem("en_made")
        rotated = sem("rotated")
        part_hi_made = sem("part_hi_made")
        part_lo_made = sem("part_lo_made")
        q_a_turned = sem("q_a_turned")
        q_hi_made = sem("q_hi_made")
        q_lo_made = sem("q_lo_made")
        q_doubled = sem("q_doubled")
        relu_made = sem("relu_made")
        relu_used = sem("relu_used")
        conv_done = sem("conv_done")
        qk_b_ready = sem("qk_b_ready")
        decay_made = sem("decay_made")
        decay_cut = sem("decay_cut")
        sp_made = sem("sp_made")
        cell_made = sem("cell_made")
        gate_t_made = sem("gate_t_made")
        bo_scaled = sem("bo_scaled")
        zt_made = sem("zt_made")
        z_made = sem("z_made")
        probs_made = sem("probs_made")
        probs_t_made = sem("probs_t_made")
        o_a_made = sem("o_a_made")
        b_var_made = sem("b_var_made")
        b_root = sem("b_root")
        zg_scaled = sem("zg_scaled")
        b_normed = sem("b_normed")
        gated_made = sem("gated_made")
        o_hi = sem("o_hi")
        o_lo = sem("o_lo")
        pad_made = sem("pad_made")
        eps_made = sem("eps_made")
        sig_made = sem("sig_made")
        sig_used = sem("sig_used")
        branch_full = sem("branch_full")
        merged = sem("merged")
        m_hi_made = sem("m_hi_made")
        m_lo_made = sem("m_lo_made")
        y_added = sem("y_added")
        y_squared = sem("y_squared")
        y_ms = sem("y_ms")
        y_root = sem("y_root")
        y_rstd = sem("y_rstd")
        y_gained = sem("y_gained")
        y_scaled = sem("y_scaled")
        y_scaled_act = sem("y_scaled_act")
        stored = [sem(f"stored{b}") for b in range(2)]
        dve_step = sem("dve_step")
        act_step = sem("act_step")
        pool_step = sem("pool_step")

        block = ctx.enter_context(nc.Block())

        def slot_pos(n):
            if n < GATE0:
                return n % SPLIT
            if n < OUT0:
                return (GATE0 + 3 * ((n - GATE0) // 3 % 2) + (n - GATE0) % 3) % SPLIT
            if n == LAST_PLACE:
                return SPLIT
            return (n - OUT0 + GATE0 + 6 - (n > LAST_PLACE)) % SPLIT

        def split_slot(n):
            p = slot_pos(n)
            return (w_last[0][:, :], w_last[1][:, :]) if p == SPLIT else (w_hi[:, p, :], w_lo[:, p, :])

        def raw_place(n):
            return n % RAW if n < LATE0 else RAW + n - LATE0

        def raw_slot(n):
            return w_raw[:, n % RAW, :] if n < LATE0 else w_late[n - LATE0][:, :]

        def slot_before(n):
            for m in range(n - 1, -1, -1):
                if slot_pos(m) == slot_pos(n):
                    return m
            return None

        def out_bank(m):
            return (len(UNITS) + 2 * KT + m) % 2

        def wait_lo(eng, n):
            if n in DVE_SLOTS:
                eng.wait_ge(lo_by_dve, DVE_SLOTS.index(n) + 1)
            else:
                eng.wait_ge(lo_by_pool, sum(1 for m in range(n + 1) if m not in DVE_SLOTS))

        def remainder(eng, n):
            eng.wait_ge(hi_made, n + 1)
            m = slot_size(n)
            hi, lo = split_slot(n)
            eng.tensor_tensor(lo[:, 0:m], raw_slot(n)[:, 0:m], hi[:, 0:m].bitcast(F32), ALU.subtract).then_inc(lo_by_dve if n in DVE_SLOTS else lo_by_pool, 1)

        def slot_size(n):
            return KT * SMALL if n == 0 else SLOT

        def bank_of(job):
            return BANKS[RING_OF[job[0]]][BANK[job]]

        def wait_full(eng, job):
            eng.wait_ge(side_done, ORDER[job] + 1)

        def wait_read(eng, job):
            kind = job[0]
            if kind == "small_tok":
                eng.wait_ge(small_copied, 1)
            elif kind == "ik_chan":
                eng.wait_ge(ik_lo_made, 1)
            elif kind == "gate_rows":
                eng.wait_ge(rows_read, 2 - job[1])
            elif kind == "gate_cols":
                eng.wait_ge(gate_tok_made, 1)
            elif kind == "stage_chan":
                if STAGED[job[1]][0] == "aq":
                    eng.wait_ge(q_a_turned, job[1] - N_IQ + 1)
                else:
                    eng.wait_ge(part_lo_made, 2 * part_unit(job) + 2)
            elif kind == "score":
                eng.wait_ge(relu_made, job[1] + 1)
            elif kind == "decay_rows":
                eng.wait_ge(decay_cut, (job[1] + 1) * TILES)
            elif kind == "qk_b":
                eng.wait_ge(sp_made, job[1] * TILES + job[2] + 1)
            elif kind == "pv_b":
                eng.wait_ge(cell_made, job[1] * TILES + job[2] + 1)
            elif kind == "qk_a":
                eng.wait_ge(z_made, job[1] + 1)
            elif kind == "probs_chan":
                eng.wait_ge(probs_t_made, job[1] + 1)
            elif kind == "pv_a":
                eng.wait_ge(o_a_made, ATTN[job[1]][0] + 1)
            else:
                eng.wait_ge(o_lo, OUT_ORDER.index(job) + 1)

        def wait_unit_read(eng, u):
            if u >= len(UNITS) + 2 * KT:
                eng.wait_ge(y_added, u - len(UNITS) - 2 * KT + 1)
            elif u >= len(UNITS):
                eng.wait_ge(sig_made, u - len(UNITS) + 1)
            elif UNITS[u][0] == "bo":
                eng.wait_ge(gate_t_made, UNITS[u][1] + 1)
            elif UNITS[u][0] in ("bz", "az"):
                eng.wait_ge(zt_made, u - UNIT[("bz", 0)] + 1)
            else:
                eng.wait_ge(unit_out, u + 1)

        def wait_slot_used(eng, n):
            if n < N_SMALL_SLOTS:
                eng.wait_ge(unit_full, 1)
            elif n < GATE0:
                g, q = divmod(n - N_SMALL_SLOTS, 4)
                if q < 3:
                    eng.wait_ge(slot_used, 3 * g + q + 1)
                else:
                    eng.wait_ge(unit_full, max(u for u, v in enumerate(UNITS) if v[0] == GROUPS[g]) + 1)
            elif n < OUT0:
                c, q = divmod(n - GATE0, 3)
                if q < 2:
                    eng.wait_ge(unit_full, len(UNITS) + 2 * c + q + 1)
                else:
                    eng.wait_ge(branch_full, 2 * c + 2)

        def part(job, e):
            g, j = STAGED[job[1]]
            same, other = slice(e * A_DIM, (e + 1) * A_DIM), slice((1 - e) * A_DIM, (2 - e) * A_DIM)
            src = bank_of(job)[same, :].rearrange("p (b t) -> p b t", t=P)
            if g == "ak":
                cols = slice(j * P, (j + 1) * P)
                return src, k_parts[same, e, :, cols], k_parts[other, e, :, cols]
            b0 = 0 if g == "iq0" else 4
            cols = slice((j - 1) * P, j * P)
            return src, iq_parts[same, e, b0:b0 + 4, cols], iq_parts[other, e, b0:b0 + 4, cols]

        def part_unit(job):
            return job[1] if job[1] < N_IQ else job[1] - TILES

        def unit_slots(u):
            g, j = UNITS[u]
            if g == "small":
                return []
            n = group_slot(g) + 4
            if g in ("iq0", "iq1"):
                return {3: [n, n + 1], 2: [n + 2], 1: [n + 3]}[j]
            if g == "az":
                return [n + j] if j < 3 else []
            return [n + j]

        def slots_quarter(u):
            if u == UNIT[("iq0", 3)]:
                return 0
            return 1 if u + 1 < len(UNITS) and UNITS[u + 1][0] != UNITS[u][0] else -1

        @block.sync
        def _(sp):
            w_in_k = w_in.rearrange("(k p) n -> p k n", p=P)
            wa_k = w_branch_a.rearrange("(k p) n -> p k n", p=P)
            wb_k = w_branch_b.rearrange("(k p) n -> p k n", p=P)
            x_t = x.rearrange("(t p) d -> p t d", p=P)
            for j in range(TILES):
                sp.dma_start(x_tok[:, j, :], x_t[:, j, :]).then_inc(x_in[j], 16)

            def load(n):
                r = raw_place(n)
                if RAW <= n < LATE0:
                    wait_lo(sp, n - RAW)
                raw = raw_slot(n)
                if n == 0:
                    small = raw[:, 0:KT * SMALL].rearrange("p (k n) -> p k n", n=SMALL)
                    sp.dma_start(small[:, :, 0:SMALL_A], w_in_k[:, :, COL["ik"]:COL["ik"] + SMALL_A])\
                        .then_inc(raw_in[r], 16)
                    sp.dma_start(small[:, :, SMALL_A:SMALL], w_in_k[:, :, COL["bi"]:COL["bi"] + 2 * B_HEADS])\
                        .then_inc(raw_in[r], 16)
                elif n < GATE0:
                    g, q = divmod(n - N_SMALL_SLOTS, 4)
                    c = GROUP_COL[GROUPS[g]]
                    sp.dma_start(raw.rearrange("p (k n) -> p k n", n=WIDTH),
                                 w_in_k[:, 2 * q:2 * q + 2, c:c + WIDTH]).then_inc(raw_in[r], 16)
                elif n < OUT0:
                    c, q = divmod(n - GATE0, 3)
                    dst = raw.rearrange("p (k n) -> p k n", n=P)
                    if q < 2:
                        col = COL["ga" if q == 0 else "gb"] + c * P
                        sp.dma_start(dst, w_in_k[:, :, col:col + P]).then_inc(raw_in[r], 16)
                    else:
                        sp.dma_start(dst[:, 0:KW, :], wa_k[:, :, c * P:(c + 1) * P]).then_inc(raw_in[r], 16)
                        sp.dma_start(dst[:, KW:2 * KW, :], wb_k[:, :, c * P:(c + 1) * P]).then_inc(raw_in[r], 16)
                else:
                    k = n - OUT0
                    sp.dma_start(raw, w_out[k * P:(k + 1) * P, :]).then_inc(raw_in[r], 16)

            for n in range(LATE0):
                if n == OUT0:
                    wait_full(sp, LAST_SIDE)
                    for late in range(LATE0, N_SLOTS):
                        load(late)
                load(n)
                if n == RAW - 1:
                    sp.dma_start(rope[:, :, :, :], rope_d.rearrange("(t p) a d -> p t a d", p=P)).then_inc(late_in, 16)
                    sp.dma_start(gate_bias[:, 0:B_HEADS], b_igate.partition_broadcast(P)).then_inc(late_in, 16)
                    sp.dma_start(gate_bias[:, B_HEADS:2 * B_HEADS], b_fgate.partition_broadcast(P)).then_inc(late_in, 16)
                    sp.dma_start(conv_b_col[:, :], conv_b).then_inc(late_in, 16)
                    sp.dma_start(conv_w_col[:, :, :], conv_w).then_inc(late_in, 16)
                if n == group_slot("bo"):
                    sp.wait_ge(relu_used, len(SCORES))
                    sp.dma_start(norm_b_row[:, :], head_norm_g.partition_broadcast(P)).then_inc(norm_row_in, 16)
            wait_slot_used(sp, OUT0 - 2)
            sp.dma_start(x_again[:, :, :], x_t).then_inc(x_again_in, 16)
            sp.wait_ge(branch_full, 2 * KT)
            sp.dma_start(final_row[:, :], final_norm_g.partition_broadcast(P)).then_inc(final_row_in, 16)
            out_t = out.rearrange("(t p) d -> p t d", p=P)
            for i in range(TILES):
                sp.wait_ge(y_scaled, i + 1)
                sp.dma_start(out_t[:, i, 0:WIDTH], y_norm[:, i % 2, 0:WIDTH]).then_inc(stored[i % 2], 16)
            for b in range(2):
                sp.wait_ge(stored[b], 32 * TILES // 2)

        def raw_count(n):
            def dmas(m):
                return 2 if m == 0 or (GATE0 <= m < OUT0 and (m - GATE0) % 3 == 2) else 1
            return 16 * sum(dmas(m) for m in range(n + 1) if raw_place(m) == raw_place(n))

        @block.gpsimd
        def _(pool):
            pool.memset(one_col[:, :], 1.0)
            pool.memset(eps_col[:, 0:1], EPS)
            pool.memset(eps_col[:, 1:2], 4 * EPS).then_inc(eps_made, 1)
            pool.memset(mask0, 0.0).then_inc(pool_step, 1)
            pool.wait_ge(pool_step, 1)
            pool.memset(mask0[0:CHUNK, CHUNK:P], MASKED)
            pool.memset(conv_in[:, :, 0:CONV_WIDTH], 0.0).then_inc(pad_made, 1)

            def side(p):
                for job in SIDE.get(p, []):
                    if job[0] == "qk_b":
                        h, j = job[1:]
                        e = h * TILES + j
                        pool.wait_ge(decay_made, e + 1)
                        d = decay[:, e % 2, 0:P]
                        pool.affine_select(out=d, in_=d, compare_op=ALU.is_ge, fill=0.0, base=0,
                                           pattern=[[1, P]], channel_multiplier=-1).then_inc(decay_cut, 1)

            for n in range(N_SMALL_SLOTS, N_SMALL_SLOTS + 4):
                remainder(pool, n)
            for u, (g, j) in enumerate(UNITS):
                if slots_quarter(u) < 0:
                    for n in unit_slots(u):
                        remainder(pool, n)
                for q in range(4):
                    side(4 * u + q)
                    if q == slots_quarter(u):
                        for n in unit_slots(u):
                            remainder(pool, n)
                if (g, j) == ("bq", 0):
                    wait_full(pool, ("score", len(SCORES) - 1))
                    pool.memset(v_b[:, :, :, B_DIM:B_DIM + 1], 1.0).then_inc(v_ones_made, 1)
                if g == "bz":
                    if j == 0:
                        pool.wait_ge(norm_row_in, 16)
                    pool.wait_ge(zt_made, j + 1)
                    pool.tensor_tensor(gated[:, j % 2, :], gated[:, j % 2, :], norm_b_row[:, :], ALU.mult)\
                        .then_inc(zg_scaled, 1)
            for c in range(KT):
                for n in range(GATE0 + 3 * (c + 1), GATE0 + 3 * (c + 2)):
                    if n not in DVE_SLOTS:
                        remainder(pool, n)
                if c == KT - 1:
                    for n in range(OUT0 + 3, N_SLOTS):
                        if n not in DVE_SLOTS:
                            remainder(pool, n)
                pool.wait_ge(m_hi_made, c + 1)
                pool.tensor_tensor(m_lo[:, c, :], prod[:, c % 2, 0, :], m_hi[:, c, :].bitcast(F32), ALU.subtract)\
                    .then_inc(m_lo_made, 1)

        @block.scalar
        def _(act):
            steps = [0]

            def link(ins):
                steps[0] += 1
                ins.then_inc(act_step, 1)
                act.wait_ge(act_step, steps[0])

            act.dma_start(ident[:, :], ident_d).then_inc(const_in, 16)
            act.dma_start(norm_col[:, :], norm_g).then_inc(const_in, 16)
            act.wait_ge(eps_made, 1)
            link(act.activation(rstd[:, 0:1], eps_col[:, 0:1], ACT.Sqrt))

            for j in range(TILES):
                act.wait_ge(x_in[j], 16)
                act.activation(x_norm[:, j, :], x_tok[:, j, :], ACT.Square, accum_out=sumsq[:, j:j + 1])\
                    .then_inc(x_squared, 1)
                act.wait_ge(x_squared, j + 1)
                act.activation(rstd[:, j:j + 1], sumsq[:, j:j + 1], ACT.Sqrt, bias=eps_col[:, 0:1],
                               scale=1.0 / D_MODEL).then_inc(x_root, 1)

            def round_slot(n):
                act.wait_ge(raw_in[raw_place(n)], raw_count(n))
                if n == LAST_PLACE:
                    act.wait_ge(branch_full, 2 * KT - 1)
                elif slot_before(n) is not None:
                    wait_slot_used(act, slot_before(n))
                m = slot_size(n)
                act.activation(split_slot(n)[0][:, 0:m], raw_slot(n)[:, 0:m], ACT.Copy).then_inc(hi_made, 1)

            round_slot(0)
            act.wait_ge(const_in, 32)
            for k in range(KT):
                act.wait_ge(x_turned, k + 1)
                act.activation(h_hi[:, k, :], start_banks[k][:, :], ACT.Copy, scale=norm_col[:, k:k + 1])\
                    .then_inc(h_hi_made, 1)
                if k in (1, 4, 7):
                    round_slot(1 + k // 3)
            round_slot(4)

            def job_side(job):
                kind = job[0]
                if kind == "ik_chan":
                    wait_full(act, job)
                    act.activation(ik_hi[:, :], bank_of(job)[:, :], ACT.Copy).then_inc(ik_hi_made, 1)
                elif kind == "small_tok":
                    act.wait_ge(gate_in, 1)
                    link(act.activation(gate_t[:, :, :], gate_t[:, :, :], ACT.Exp, scale=-1.0))
                    act.activation(gate_t[:, :, :], gate_t[:, :, :], ACT.Ln, bias=one_col[:, 0:1])\
                        .then_inc(gate_ln, 1)
                elif kind == "gate_cols":
                    act.wait_ge(gate_tok_made, 1)
                    act.activation(en_m[:, :, :], gate_tok[:, 1, :, :], ACT.Exp).then_inc(en_made, 1)
                elif kind == "stage_chan" and STAGED[job[1]][0] == "aq":
                    j = STAGED[job[1]][1]
                    wait_full(act, job)
                    act.activation(q_a[:, :, j * P:(j + 1) * P],
                                   bank_of(job)[:, :].rearrange("p (b t) -> p b t", t=P), ACT.Copy)\
                        .then_inc(q_a_turned, 1)
                elif kind == "stage_chan":
                    if STAGED[job[1]] == ("ak", 0):
                        act.wait_ge(gate_tok_made, 1)
                    wait_full(act, job)
                    for e in range(2):
                        src, hi, _ = part(job, e)
                        act.activation(hi, src, ACT.Copy).then_inc(part_hi_made, 1)
                elif kind == "score":
                    s = job[1]
                    i, h = SCORES[s]
                    w = (i + 1) * P
                    wait_full(act, job)
                    if s >= RELUS:
                        act.wait_ge(relu_used, s - RELUS + 1)
                    act.activation(relu[:, s % RELUS, 0:w], bank_of(job)[:, 0:w], ACT.Relu,
                                   scale=float(IDX_DIM) ** -0.5).then_inc(relu_made, 1)
                elif kind == "qk_b":
                    h, j = job[1:]
                    e = h * TILES + j
                    rows = ("decay_rows", h)
                    if j == 0:
                        wait_full(act, rows)
                    if e >= 2:
                        act.wait_ge(sp_made, e - 1)
                    act.activation(decay[:, e % 2, 0:SEQ - j * P], bank_of(rows)[:, j * P:SEQ], ACT.Exp,
                                   bias=gate_tok[:, 0, j, h:h + 1]).then_inc(decay_made, 1)
                elif kind == "pv_b":
                    h, i = job[1:]
                    wait_full(act, job)
                    act.activation(cell[:, i, h, :], bank_of(job)[:, 0:B_DIM + 1], ACT.Copy)\
                        .then_inc(cell_made, 1)
                elif kind == "qk_a":
                    s = job[1]
                    w = (ATTN[s][0] + 1) * P
                    act.wait_ge(z_made, s + 1)
                    act.activation(probs[:, s % 2, 0:w], probs[:, s % 2, 0:w], ACT.Exp, scale=-1.0,
                                   bias=neg_max[:, s:s + 1], accum_out=p_sum[:, s:s + 1])\
                        .then_inc(probs_made, 1)
                elif kind in ("out_a_chan", "out_b_chan"):
                    j = job[1]
                    dst = oa_hi if kind == "out_a_chan" else ob_hi
                    wait_full(act, job)
                    act.activation(dst[:, :, j * P:(j + 1) * P],
                                   bank_of(job)[:, :].rearrange("p (b t) -> p b t", t=P), ACT.Copy, scale=0.5)\
                        .then_inc(o_hi, 1)

            def evacuate(u):
                g, j = UNITS[u]
                src = pj[u % 2]
                done = unit_out
                act.wait_ge(unit_full, u + 1)
                if g == "small":
                    act.activation(small_chan[:, :], src[0:SMALL, :], ACT.Copy).then_inc(done, 1)
                elif g in ("iq0", "iq1", "aq", "ak"):
                    n = STAGED.index((g, j))
                    if n >= 2:
                        old = ("stage_chan", n - 2)
                        wait_full(act, old)
                    act.activation(stage[:, n % 2, :], src[:, :], ACT.Copy).then_inc(done, 1)
                elif g in CHAN_GROUPS:
                    b = j + (0 if g == "bq" else B_HEADS)
                    if b == 0:
                        wait_full(act, ("stage_chan", len(STAGED) - 1))
                        act.wait_ge(late_in, 16 * 5)
                    if b >= 2:
                        act.wait_ge(conv_done, b - 1)
                    act.activation(conv_in[:, b % 2, CONV_WIDTH:], src[:, :], ACT.Copy)
                    if b >= 2:
                        act.wait_ge(qk_b_ready, b - 1)
                    act.activation(conv_acc[:, b % 2, :], src[:, :], ACT.Identity,
                                   scale=conv_w_col[:, b, CONV_WIDTH - 1:CONV_WIDTH],
                                   bias=conv_b_col[:, b:b + 1]).then_inc(done, 1)
                elif g == "bv":
                    act.activation(v_b[:, j, :, 0:B_DIM], src[:, :].rearrange("p (h d) -> p h d", d=B_DIM), ACT.Copy)\
                        .then_inc(done, 1)
                elif g == "av":
                    act.activation(v_a[:, j, :], src[:, :], ACT.Copy).then_inc(done, 1)
                else:
                    n = 4 * ("bo", "bz", "az").index(g) + j
                    if 2 <= n < 2 + TILES:
                        act.wait_ge(bo_scaled, n - 1)
                    elif n >= 2 + TILES:
                        act.wait_ge(zt_made, n - 1 - TILES)
                    act.activation(gate_ring[n % 2][:, :], src[:, :], ACT.Tanh, scale=0.5).then_inc(gate_t_made, 1)

            def split_queries(i):
                if i == 0:
                    wait_full(act, ("pv_b", B_HEADS - 1, TILES - 1))
                if i >= 2:
                    wait_full(act, ("qk_a", A_HEADS * (i - 1) - 1))
                act.wait_ge(q_a_turned, i + 1)
                for e in range(2):
                    same = slice(e * A_DIM, (e + 1) * A_DIM)
                    act.activation(q_twice[same, i % 2, e, :, :], q_a[same, :, i * P:(i + 1) * P], ACT.Copy)\
                        .then_inc(q_hi_made, 1)
                for e in range(2):
                    same, other = slice(e * A_DIM, (e + 1) * A_DIM), slice((1 - e) * A_DIM, (2 - e) * A_DIM)
                    act.activation(q_twice[other, i % 2, e, :, :], q_a[same, :, i * P:(i + 1) * P], ACT.Copy)\
                        .then_inc(q_doubled, 1)

            def silu_conv(b):
                act.wait_ge(conv_done, b + 1)
                act.activation(qk_b[:, b, :], conv_acc[:, b % 2, :], ACT.Silu).then_inc(qk_b_ready, 1)

            for u, (g, j) in enumerate(UNITS):
                if slots_quarter(u) < 0:
                    for n in unit_slots(u):
                        round_slot(n)
                for q in range(4):
                    if q == 3:
                        evacuate(u)
                    if 4 * u + q in SPLIT_AT:
                        split_queries(SPLIT_AT[4 * u + q])
                    for job in SIDE.get(4 * u + q, []):
                        job_side(job)
                    if q == slots_quarter(u):
                        for n in unit_slots(u):
                            round_slot(n)
                    if q == 3 and UNITS[u - 1][0] in CHAN_GROUPS:
                        b = UNITS[u - 1][1] + (0 if UNITS[u - 1][0] == "bq" else B_HEADS)
                        silu_conv(b)
                if (g, j) == ("bz", 0):
                    act.wait_ge(b_var_made, TILES)
                    act.activation(b_rstd[:, :, :], mean_var[:, :, :, 1], ACT.Sqrt, bias=eps_col[:, 1:2])\
                        .then_inc(b_root, 1)

            for c in range(KT):
                for n in range(GATE0 + 3 * (c + 1), GATE0 + 3 * (c + 2)):
                    round_slot(n)
                for s in range(2):
                    if c == KT - 1:
                        round_slot(OUT0 + 3 + s)
                    u = len(UNITS) + 2 * c + s
                    act.wait_ge(unit_full, u + 1)
                    if c >= 2:
                        act.wait_ge(sig_used, 2 * (c - 2) + s + 1)
                    if c == 0 and s == 0:
                        act.wait_ge(gated_made, 2 * TILES)
                    act.activation(sig[:, c % 2, s, :], pj[u % 2][:, :], ACT.Sigmoid).then_inc(sig_made, 1)
                    if c == 0 and s == 0:
                        job_side(LAST_SIDE)
                if c == KT - 1:
                    for n in range(OUT0 + 5, N_SLOTS):
                        round_slot(n)
                act.wait_ge(merged, c + 1)
                act.activation(m_hi[:, c, :], prod[:, c % 2, 0, :], ACT.Copy).then_inc(m_hi_made, 1)
            for m, (i, piece, cols) in enumerate(OUT_UNITS):
                width = cols.stop - cols.start
                act.wait_ge(y_added, m + 1)
                if m >= 2:
                    act.wait_ge(y_squared, m - 1)
                act.activation(square[:, m % 2, 0:width], y_tok[:, i % 2, cols], ACT.Square,
                               accum_out=out_sq[:, i, piece:piece + 1]).then_inc(y_squared, 1)
                if cols.stop == D_MODEL:
                    act.wait_ge(y_squared, m + 1)
                    act.wait_ge(y_ms, i + 1)
                    act.activation(out_rstd[:, i:i + 1], out_sq[:, i, piece:piece + 1], ACT.Sqrt,
                                   bias=out_ms[:, i:i + 1], scale=1.0 / D_MODEL).then_inc(y_root, 1)
                    act.wait_ge(y_rstd, i + 1)
                    act.wait_ge(y_gained, m + 1)
                    half = y_norm[:, i % 2, WIDTH:D_MODEL]
                    act.activation(half, half, ACT.Copy, scale=out_rstd[:, i:i + 1]).then_inc(y_scaled_act, 1)
                    act.wait_ge(y_scaled_act, i + 1)
                    act.dma_start(out.rearrange("(t p) d -> p t d", p=P)[:, i, WIDTH:D_MODEL], half)\
                        .then_inc(stored[i % 2], 16)

        @block.vector
        def _(dve):
            steps = [0]

            def link(ins):
                steps[0] += 1
                ins.then_inc(dve_step, 1)
                dve.wait_ge(dve_step, steps[0])

            for j in range(TILES):
                dve.wait_ge(x_root, j + 1)
                link(dve.reciprocal(rstd[:, j:j + 1], rstd[:, j:j + 1]))
                dve.tensor_scalar(x_norm[:, j, :], x_tok[:, j, :], rstd[:, j:j + 1], None, ALU.mult)\
                    .then_inc(x_scaled, 1)
            remainder(dve, 0)
            dve.wait_ge(const_in, 32)
            for k in range(KT):
                dve.wait_ge(h_hi_made, k + 1)
                dve.scalar_tensor_tensor(out=h_lo[:, k, :], in0=start_banks[k][:, :], scalar=norm_col[:, k:k + 1],
                                         in1=h_hi[:, k, :].bitcast(F32), op0=ALU.mult, op1=ALU.subtract)\
                    .then_inc(h_lo_made, 1)
            dve.wait_ge(late_in, 16 * 5)

            def rotate(dst, src, tmp, cos, sin):
                link(dve.tensor_tensor(tmp[..., 0:HALF], src[..., HALF:ROT], sin[..., 0:HALF], ALU.mult))
                link(dve.tensor_tensor(tmp[..., HALF:ROT], src[..., 0:HALF], sin[..., HALF:ROT], ALU.mult))
                link(dve.tensor_tensor(dst[..., 0:ROT], src[..., 0:ROT], cos, ALU.mult))
                return dve.tensor_tensor(dst[..., 0:ROT], dst[..., 0:ROT], tmp, ALU.add)

            def absolute(dst, src):
                return dve.scalar_tensor_tensor(out=dst, in0=src, scalar=-1.0, in1=src, op0=ALU.mult, op1=ALU.max)

            def small(job):
                wait_full(dve, job)
                dve.tensor_copy(small_tok[:, :, :],
                                bank_of(job)[:, 0:TILES * SMALL].rearrange("p (t n) -> p t n", n=SMALL))\
                    .then_inc(small_copied, 1)
                dve.wait_ge(small_copied, 1)
                link(dve.tensor_tensor(gate_x[:, :, :], small_tok[:, :, SMALL_A:SMALL],
                                       gate_bias[:, :].unsqueeze(1).to_broadcast([P, TILES, 2 * B_HEADS]), ALU.add))
                absolute(gate_t[:, :, :], gate_x[:, :, B_HEADS:2 * B_HEADS]).then_inc(gate_in, 1)
                link(rotate(small_tok[:, :, 0:ROT], small_tok[:, :, 0:ROT], small_t[:, :, :],
                            rope[:, :, 0, :], rope[:, :, 1, :]))
                link(dve.tensor_copy(ik_twice[:, :, 0:IDX_DIM], small_tok[:, :, 0:IDX_DIM]))
                dve.tensor_copy(ik_twice[:, :, IDX_DIM:P], small_tok[:, :, 0:IDX_DIM]).then_inc(ik_ready, 1)
                dve.tensor_scalar(idx_w[:, :, :], small_tok[:, :, IDX_DIM:SMALL_A], float(IDX_HEADS) ** -0.5,
                                  None, ALU.mult)
                link(dve.tensor_copy(gate_l[:, :, 0:B_HEADS], gate_x[:, :, 0:B_HEADS]))
                link(dve.tensor_scalar(gate_l[:, :, B_HEADS:], gate_x[:, :, B_HEADS:], 0.0, None, ALU.min))

            def forget_log():
                dve.wait_ge(gate_ln, 1)
                dve.tensor_tensor(gate_l[:, :, B_HEADS:], gate_l[:, :, B_HEADS:], gate_t[:, :, :], ALU.subtract)\
                    .then_inc(gate_logs, 1)

            def rows(job):
                if job[1] == 1:
                    return
                li, lf = ("gate_rows", 0), ("gate_rows", 1)
                wait_full(dve, li)
                ones = one_col[0:B_HEADS, 0:1].to_broadcast([B_HEADS, SEQ])
                dve.tensor_tensor_scan(f_row[:, :], ones, bank_of(lf)[0:B_HEADS, :], 0.0, ALU.mult, ALU.add)\
                    .then_inc(rows_read, 1)
                dve.wait_ge(rows_read, 1)
                dve.tensor_tensor(a_row[:, :], bank_of(li)[0:B_HEADS, :], f_row[:, :], ALU.subtract)\
                    .then_inc(rows_read, 1)
                dve.wait_ge(rows_read, 2)
                link(dve.tensor_tensor_scan(nm_row[:, :], a_row[:, :], a_row[:, :], 0.0, ALU.max, ALU.max))
                link(dve.tensor_scalar(neg_m_hi[:, :], nm_row[:, :], -1.0, None, ALU.mult))
                link(dve.scalar_tensor_tensor(out=neg_m_lo[:, :], in0=nm_row[:, :], scalar=-1.0,
                                              in1=neg_m_hi[:, :].bitcast(F32), op0=ALU.mult, op1=ALU.subtract))
                dve.tensor_copy(head_row[:, :], ident[0:B_HEADS, 0:B_HEADS])
                dve.scalar_tensor_tensor(out=nm_row[:, :], in0=nm_row[:, :], scalar=-1.0, in1=f_row[:, :],
                                         op0=ALU.mult, op1=ALU.subtract).then_inc(rows_ready, 1)

            def score_step(job):
                s = job[1]
                i, h = SCORES[s]
                w = (i + 1) * P
                acc = score[:, i - 1, 0:w]
                dve.wait_ge(relu_made, s + 1)
                wt = idx_w[:, i, h:h + 1]
                if h == 0:
                    ins = dve.tensor_scalar(acc, relu[:, s % RELUS, 0:w], wt, None, ALU.mult)
                else:
                    dve.wait_ge(relu_used, s)
                    ins = dve.scalar_tensor_tensor(out=acc, in0=relu[:, s % RELUS, 0:w], scalar=wt, in1=acc,
                                                   op0=ALU.mult, op1=ALU.add)
                ins.then_inc(relu_used, 1)
                if h == IDX_HEADS - 1:
                    dve.wait_ge(relu_used, s + 1)
                    link(dve.memset(score[0:CHUNK, i - 1, w - CHUNK:w], NO_KEY))

            def top_round(i, r):
                w = (i + 1) * P
                acc = score[:, i - 1, 0:w]
                link(dve.max(top8[:, i, :], acc))
                link(dve.match_replace(acc, top8[:, i, :], acc, TAKEN))
                if r == ROUNDS - 1:
                    link(dve.tensor_scalar(acc, acc, BETWEEN, MASKED, ALU.is_gt, ALU.mult))

            def conv(b):
                if b == 0:
                    dve.wait_ge(pad_made, 1)
                wait_unit_read(dve, UNIT[("bq", 0)] + b)
                for t in range(CONV_WIDTH - 1):
                    ins = dve.scalar_tensor_tensor(
                        out=conv_acc[:, b % 2, :], in0=conv_in[:, b % 2, t + 1:t + 1 + SEQ],
                        scalar=conv_w_col[:, b, t:t + 1], in1=conv_acc[:, b % 2, :], op0=ALU.mult, op1=ALU.add)
                    if t < CONV_WIDTH - 2:
                        link(ins)
                ins.then_inc(conv_done, 1)

            def packed(j):
                return P * (TILES * j - j * (j - 1) // 2)

            def job_side(job):
                kind = job[0]
                if kind == "small_tok":
                    small(job)
                elif kind == "gate_rows":
                    rows(job)
                elif kind == "gate_cols":
                    wait_full(dve, job)
                    dve.tensor_copy(gate_tok[:, :, :, :].rearrange("p a t h -> p (a t h)"),
                                    bank_of(job)[:, 0:2 * TILES * B_HEADS]).then_inc(gate_tok_made, 1)
                elif kind == "ik_chan":
                    dve.wait_ge(ik_hi_made, 1)
                    dve.tensor_tensor(ik_lo[:, :], bank_of(job)[:, :], ik_hi[:, :].bitcast(F32), ALU.subtract)\
                        .then_inc(ik_lo_made, 1)
                elif kind == "stage_chan" and STAGED[job[1]][0] != "aq":
                    for e in range(2):
                        src, hi, lo = part(job, e)
                        dve.wait_ge(part_hi_made, 2 * part_unit(job) + e + 1)
                        dve.tensor_tensor(lo, src, hi.bitcast(F32), ALU.subtract).then_inc(part_lo_made, 1)
                elif kind == "score":
                    score_step(job)
                elif kind == "qk_b":
                    h, j = job[1:]
                    e = h * TILES + j
                    w = SEQ - j * P
                    wait_full(dve, job)
                    dve.wait_ge(decay_cut, e + 1)
                    if h >= 2 and j == 0:
                        wait_full(dve, ("pv_b", h - 2, TILES - 1))
                    dve.scalar_tensor_tensor(out=sp[:, h % 2, packed(j):packed(j) + w], in0=bank_of(job)[:, 0:w],
                                             scalar=float(B_DIM) ** -0.5, in1=decay[:, e % 2, 0:w],
                                             op0=ALU.mult, op1=ALU.mult).then_inc(sp_made, 1)
                elif kind == "qk_a":
                    s = job[1]
                    i, h = ATTN[s]
                    w = (i + 1) * P
                    mask = mask0 if i == 0 else score[:, i - 1, 0:w]
                    wait_full(dve, job)
                    if s >= 2:
                        wait_full(dve, ("probs_chan", s - 2))
                    dve.tensor_tensor_reduce(out=probs[:, s % 2, 0:w], in0=bank_of(job)[:, 0:w], in1=mask,
                                             scale=-float(A_DIM) ** -0.5, scalar=3.0e38, op0=ALU.add, op1=ALU.min,
                                             accum_out=neg_max[:, s:s + 1]).then_inc(z_made, 1)
                elif kind == "probs_chan":
                    s = job[1]
                    w = (ATTN[s][0] + 1) * P
                    wait_full(dve, job)
                    if s >= 2:
                        wait_full(dve, ("pv_a", s - 2))
                    dve.tensor_copy(probs_t[:, s % 2, 0:w], bank_of(job)[:, 0:w]).then_inc(probs_t_made, 1)
                elif kind == "pv_a":
                    s = job[1]
                    i, h = ATTN[s]
                    if h == A_HEADS - 1:
                        wait_full(dve, job)
                        dve.wait_ge(probs_made, s + 1)
                        rec = p_rec[:, s - h:s + 1]
                        link(dve.reciprocal(rec, p_sum[:, s - h:s + 1]))
                        dve.tensor_tensor(o_a[:, i, :].rearrange("p (h d) -> p h d", d=A_DIM),
                                          bank_of(job)[:, :].rearrange("p (h d) -> p h d", d=A_DIM),
                                          rec.unsqueeze(2).to_broadcast([P, A_HEADS, A_DIM]), ALU.mult)\
                            .then_inc(o_a_made, 1)
                elif kind in ("out_a_chan", "out_b_chan"):
                    j = job[1]
                    n = OUT_ORDER.index(job)
                    hi, lo = (oa_hi, oa_lo) if kind == "out_a_chan" else (ob_hi, ob_lo)
                    dve.wait_ge(o_hi, n + 1)
                    dve.scalar_tensor_tensor(
                        out=lo[:, :, j * P:(j + 1) * P], in0=bank_of(job)[:, :].rearrange("p (b t) -> p b t", t=P),
                        scalar=0.5, in1=hi[:, :, j * P:(j + 1) * P].bitcast(F32), op0=ALU.mult, op1=ALU.subtract)\
                        .then_inc(o_lo, 1)

            def split_queries(i):
                for e in range(2):
                    same = slice(e * A_DIM, (e + 1) * A_DIM)
                    dve.wait_ge(q_hi_made, 2 * i + e + 1)
                    hi = q_twice[same, i % 2, e, :, :]
                    dve.tensor_tensor(q_lo[same, i % 2, :, :], q_a[same, :, i * P:(i + 1) * P], hi.bitcast(F32),
                                      ALU.subtract).then_inc(q_lo_made, 1)

            def cell_scale():
                wait_read(dve, ("pv_b", B_HEADS - 1, TILES - 1))
                dve.wait_ge(en_made, 1)
                link(absolute(den[:, :, :], cell[:, :, :, B_DIM]))
                link(dve.tensor_tensor(den[:, :, :], den[:, :, :], en_m[:, :, :], ALU.max))
                link(dve.reciprocal(den[:, :, :], den[:, :, :]))

            def unit(u):
                g, j = UNITS[u]
                if g in ("iq0", "iq1", "aq", "ak"):
                    n = STAGED.index((g, j))
                    wait_unit_read(dve, u)
                    st = stage[:, n % 2, :].rearrange("p (h d) -> p h d", d=A_DIM)
                    cos = rope[:, j, 0, :].unsqueeze(1).to_broadcast([P, A_HEADS, ROT])
                    sin = rope[:, j, 1, :].unsqueeze(1).to_broadcast([P, A_HEADS, ROT])
                    rotate(st, st, rot_t[:, n % 2, :, :], cos, sin).then_inc(rotated, 1)
                    if n == 0:
                        forget_log()
                elif g in CHAN_GROUPS:
                    conv(j + (0 if g == "bq" else B_HEADS))
                elif g == "bo":
                    if j == 0:
                        cell_scale()
                    dve.wait_ge(gate_t_made, j + 1)
                    c = cell[:, j, :, 0:B_DIM]
                    link(dve.tensor_tensor(c, c, den[:, j, :].unsqueeze(2).to_broadcast([P, B_HEADS, B_DIM]), ALU.mult))
                    ins = dve.scalar_tensor_tensor(out=c, in0=gate_ring[j % 2][:, :].rearrange("p (h d) -> p h d", d=B_DIM),
                                                   scalar=1.0, in1=c, op0=ALU.add, op1=ALU.mult)
                    ins.then_inc(bo_scaled, 1)
                elif g in ("bz", "az"):
                    n = 4 * ("bo", "bz", "az").index(g) + j
                    m = n - 4
                    dve.wait_ge(gate_t_made, n + 1)
                    if m >= 2:
                        wait_full(dve, OUT_ORDER[m - 2])
                    ring = gated[:, m % 2, :]
                    ins = dve.scalar_tensor_tensor(out=ring, in0=gate_ring[n % 2][:, :], scalar=1.0,
                                                   in1=pj[u % 2][:, :], op0=ALU.add, op1=ALU.mult)
                    ins.then_inc(zt_made, 1)
                    if g == "bz":
                        if j == 0:
                            dve.wait_ge(b_root, 1)
                            link(dve.reciprocal(b_rstd[:, :, :], b_rstd[:, :, :]))
                        for h in range(B_HEADS):
                            c = cell[:, j, h, 0:B_DIM]
                            ins = dve.tensor_scalar(c, c, mean_var[:, j, h, 0:1], b_rstd[:, j, h:h + 1],
                                                    ALU.subtract, ALU.mult)
                        ins.then_inc(b_normed, 1)

            def unit_rest(u):
                g, j = UNITS[u]
                if g == "bo":
                    dve.wait_ge(bo_scaled, j + 1)
                    for h in range(B_HEADS):
                        ins = dve.bn_stats(bn6[:, h, :], cell[:, j, h, 0:B_DIM])
                    link(ins)
                    for h in range(B_HEADS):
                        ins = dve.bn_aggr(mean_var[:, j, h, :], bn6[:, h, :])
                    ins.then_inc(b_var_made, 1)
                    dve.wait_ge(b_var_made, j + 1)
                elif g == "bz":
                    ring = gated[:, j % 2, :].rearrange("p (h d) -> p h d", d=B_DIM)
                    dve.wait_ge(zg_scaled, j + 1)
                    dve.wait_ge(b_normed, j + 1)
                    dve.tensor_tensor(ring, ring, cell[:, j, :, 0:B_DIM], ALU.mult).then_inc(gated_made, 1)
                elif g == "az":
                    ring = gated[:, (TILES + j) % 2, :]
                    dve.wait_ge(zt_made, TILES + j + 1)
                    dve.tensor_tensor(ring, ring, o_a[:, j, :], ALU.mult).then_inc(gated_made, 1)

            for u in range(len(UNITS)):
                for q in range(4):
                    p = 4 * u + q
                    if p in SPLIT_AT:
                        split_queries(SPLIT_AT[p])
                    for job in SIDE.get(p, []):
                        job_side(job)
                    for i, r in TOPK_AT.get(p, []):
                        top_round(i, r)
                    if q == 0 and u > 0:
                        unit_rest(u - 1)
                unit(u)
            unit_rest(len(UNITS) - 1)

            for c in range(KT):
                if c == 0:
                    job_side(LAST_SIDE)
                if c == KT - 1:
                    for n in DVE_SLOTS[1:3]:
                        remainder(dve, n)
                for s in range(2):
                    n = 2 * c + s
                    u = len(UNITS) + n
                    if c == KT - 1 and s == 1:
                        remainder(dve, OUT0 + 6)
                    wait_unit_read(dve, u)
                    dve.wait_ge(branch_full, n + 1)
                    if c >= 2:
                        dve.wait_ge(m_lo_made, c - 1)
                    bank = (qb if s == 0 else ob)[c % 2]
                    dve.tensor_tensor(prod[:, c % 2, s, :], bank[:, :], sig[:, c % 2, s, :], ALU.mult)\
                        .then_inc(sig_used, 1)
                dve.wait_ge(sig_used, 2 * c + 2)
                dve.tensor_tensor(prod[:, c % 2, 0, :], prod[:, c % 2, 0, :], prod[:, c % 2, 1, :], ALU.add)\
                    .then_inc(merged, 1)
            remainder(dve, OUT0 + 7)

            dve.wait_ge(x_again_in, 16)
            dve.wait_ge(final_row_in, 16)
            for m, (i, piece, cols) in enumerate(OUT_UNITS):
                width = cols.stop - cols.start
                if cols.stop == D_MODEL:
                    dve.wait_ge(y_squared, m)
                    if piece == 2:
                        link(dve.tensor_tensor(out_sq[:, i, 0:1], out_sq[:, i, 0:1], out_sq[:, i, 1:2], ALU.add))
                    dve.tensor_scalar(out_ms[:, i:i + 1], out_sq[:, i, 0:1], 1.0 / D_MODEL, EPS, ALU.mult, ALU.add)\
                        .then_inc(y_ms, 1)
                dve.wait_ge(unit_full, len(UNITS) + 2 * KT + m + 1)
                if piece == 0 and i >= 2:
                    dve.wait_ge(y_scaled, i - 1)
                    dve.wait_ge(y_scaled_act, i - 1)
                    dve.wait_ge(stored[i % 2], 32)
                dve.tensor_tensor(y_tok[:, i % 2, cols], pj[out_bank(m)][:, 0:width], x_again[:, i, cols], ALU.add)\
                    .then_inc(y_added, 1)
                dve.wait_ge(y_added, m + 1)
                ins = dve.tensor_tensor(y_norm[:, i % 2, cols], y_tok[:, i % 2, cols], final_row[:, cols], ALU.mult)
                ins.then_inc(y_gained, 1)
                if cols.stop == D_MODEL:
                    dve.wait_ge(y_root, i + 1)
                    dve.reciprocal(out_rstd[:, i:i + 1], out_rstd[:, i:i + 1]).then_inc(y_rstd, 1)
                    dve.wait_ge(y_rstd, i + 1)
                    dve.wait_ge(y_gained, m + 1)
                    dve.tensor_scalar(y_norm[:, i % 2, 0:WIDTH], y_norm[:, i % 2, 0:WIDTH], out_rstd[:, i:i + 1], None,
                                      ALU.mult).then_inc(y_scaled, 1)

        @block.tensor
        def _(pe):
            def three(bank, a, b, first, last):
                (a_hi, a_lo), (b_hi, b_lo) = a, b
                pe.matmul(bank, a_hi, b_hi, start=first, stop=False)
                pe.matmul(bank, a_hi, b_lo, start=False, stop=False)
                return pe.matmul(bank, a_lo, b_hi, start=False, stop=last)

            def w_part(n, a, b):
                hi, lo = split_slot(n)
                return hi[:, a:b], lo[:, a:b]

            def h_part(k, a, b):
                return h_hi[:, k, a:b], h_lo[:, k, a:b]

            pe.wait_ge(const_in, 32)
            for j in range(TILES):
                pe.wait_ge(x_scaled, j + 1)
                for k in range(KT):
                    ins = pe.transpose(start_banks[k][:, j * P:(j + 1) * P], x_norm[:, j, k * P:(k + 1) * P], ident[:, :])
                    if j == TILES - 1:
                        ins.then_inc(x_turned, 1)

            def side(job):
                kind = job[0]
                bank = bank_of(job)
                if BEFORE[job] is not None:
                    wait_read(pe, BEFORE[job])
                if kind == "small_tok":
                    wait_unit_read(pe, 0)
                    for j in range(TILES):
                        ins = pe.transpose(bank[:, j * SMALL:(j + 1) * SMALL], small_chan[:, j * P:(j + 1) * P],
                                           ident[0:SMALL, 0:SMALL])
                elif kind == "ik_chan":
                    pe.wait_ge(ik_ready, 1)
                    for j in range(TILES):
                        ins = pe.transpose(bank[:, j * P:(j + 1) * P], ik_twice[:, j, :], ident[:, :])
                elif kind == "gate_rows":
                    pe.wait_ge(gate_logs, 1)
                    c = job[1] * B_HEADS
                    for j in range(TILES):
                        ins = pe.transpose(bank[0:B_HEADS, j * P:(j + 1) * P], gate_l[:, j, c:c + B_HEADS], ident[:, :])
                elif kind == "gate_cols":
                    pe.wait_ge(rows_ready, 1)
                    for a, row in enumerate((a_row, nm_row)):
                        for j in range(TILES):
                            c = (a * TILES + j) * B_HEADS
                            ins = pe.transpose(bank[:, c:c + B_HEADS], row[:, j * P:(j + 1) * P],
                                               ident[0:B_HEADS, 0:B_HEADS])
                elif kind == "stage_chan":
                    n = job[1]
                    pe.wait_ge(rotated, n + 1)
                    for b in range(4):
                        ins = pe.transpose(bank[:, b * P:(b + 1) * P], stage[:, n % 2, b * P:(b + 1) * P], ident[:, :])
                elif kind == "score":
                    s = job[1]
                    i, h = SCORES[s]
                    w = (i + 1) * P
                    if s == 0:
                        wait_read(pe, ("ik_chan",))
                    if s in (0, 8, 24, 40):
                        wait_read(pe, ("stage_chan", STAGED.index(("iq0" if h < 8 else "iq1", i))))
                    queries = iq_parts[:, h % 2, h // 2, (i - 1) * P:i * P]
                    pe.matmul(bank[:, 0:w], queries, ik_hi[:, 0:w], start=True, stop=False)
                    ins = pe.matmul(bank[:, 0:w], queries, ik_lo[:, 0:w], start=False, stop=True)
                elif kind == "decay_rows":
                    h = job[1]
                    one_head = head_row[:, h:h + 1].to_broadcast([B_HEADS, P])
                    pe.matmul(bank[:, :], one_head, neg_m_hi[:, :], start=True, stop=False)
                    ins = pe.matmul(bank[:, :], one_head, neg_m_lo[:, :], start=False, stop=True)
                elif kind == "qk_b":
                    h, j = job[1:]
                    if j == 0:
                        pe.wait_ge(qk_b_ready, 2 * B_HEADS if h == 0 else 1)
                    ins = pe.matmul(bank[:, 0:SEQ - j * P], qk_b[:, B_HEADS + h, j * P:(j + 1) * P],
                                    qk_b[:, h, j * P:SEQ], start=True, stop=True)
                elif kind == "pv_b":
                    h, i = job[1:]
                    wait_read(pe, ("qk_b", h, i))
                    if h == 0 and i == 0:
                        pe.wait_ge(v_ones_made, 1)
                    for j in range(i + 1):
                        c = P * (TILES * j - j * (j - 1) // 2) + (i - j) * P
                        ins = pe.matmul(bank[:, 0:B_DIM + 1], sp[:, h % 2, c:c + P], v_b[:, j, h, :],
                                        start=(j == 0), stop=(j == i))
                elif kind == "qk_a":
                    s = job[1]
                    i, h = ATTN[s]
                    w = (i + 1) * P
                    if s == 0:
                        wait_read(pe, ("stage_chan", len(STAGED) - 1))
                    if h == 0:
                        pe.wait_ge(q_doubled, 2 * (i + 1))
                        pe.wait_ge(q_lo_made, 2 * (i + 1))
                    e, b = h % 2, h // 2
                    r = slice(e * A_DIM, (e + 1) * A_DIM)
                    pe.matmul(bank[:, 0:w], q_twice[:, i % 2, e, b, :], k_parts[:, e, b, 0:w], start=True, stop=False)
                    ins = pe.matmul(bank[:, 0:w], q_lo[r, i % 2, b, :], k_parts[r, e, b, 0:w], start=False, stop=True)
                elif kind == "probs_chan":
                    s = job[1]
                    pe.wait_ge(probs_made, s + 1)
                    for j in range(ATTN[s][0] + 1):
                        ins = pe.transpose(bank[:, j * P:(j + 1) * P], probs[:, s % 2, j * P:(j + 1) * P], ident[:, :])
                elif kind == "pv_a":
                    s = job[1]
                    i, h = ATTN[s]
                    wait_read(pe, ("probs_chan", s))
                    for j in range(i + 1):
                        ins = pe.matmul(bank[:, h * A_DIM:(h + 1) * A_DIM], probs_t[:, s % 2, j * P:(j + 1) * P],
                                        v_a[:, j, h * A_DIM:(h + 1) * A_DIM], start=(j == 0), stop=(j == i))
                elif kind in ("out_a_chan", "out_b_chan"):
                    pe.wait_ge(gated_made, OUT_ORDER.index(job) + 1)
                    ring = gated[:, OUT_ORDER.index(job) % 2, :]
                    for b in range(KW):
                        ins = pe.transpose(bank[:, b * P:(b + 1) * P], ring[:, b * P:(b + 1) * P], ident[:, :])
                ins.then_inc(side_done, 1)

            for u, (g, j) in enumerate(UNITS):
                bank = pj[u % 2]
                if u >= 2:
                    wait_unit_read(pe, u - 2)
                if g == "small":
                    wait_lo(pe, 0)
                    for k in range(KT):
                        pe.wait_ge(h_lo_made, k + 1)
                        ins = three(bank[0:SMALL, :], w_part(0, k * SMALL, (k + 1) * SMALL), h_part(k, 0, SEQ),
                                    k == 0, k == KT - 1)
                    ins.then_inc(unit_full, 1)
                    continue
                units = [v for v in UNITS if v[0] == g]
                for q in range(4):
                    n = group_slot(g) + q
                    if (g, j) == units[0]:
                        wait_lo(pe, n)
                    for k in (2 * q, 2 * q + 1):
                        c = (k % 2) * WIDTH
                        if g in CHAN_GROUPS:
                            a, b = w_part(n, c + j * P, c + (j + 1) * P), h_part(k, 0, SEQ)
                        else:
                            a, b = h_part(k, j * P, (j + 1) * P), w_part(n, c, c + WIDTH)
                        ins = three(bank[:, :], a, b, k == 0, k == KT - 1)
                    if q == 3:
                        ins.then_inc(unit_full, 1)
                    elif (g, j) == units[-1]:
                        ins.then_inc(slot_used, 1)
                    for job in SIDE.get(4 * u + q, []):
                        side(job)

            for c in range(KT):
                for s in range(2):
                    u = len(UNITS) + 2 * c + s
                    n = GATE0 + 3 * c + s
                    wait_unit_read(pe, u - 2)
                    wait_lo(pe, n)
                    for k in range(KT):
                        ins = three(pj[u % 2][:, :], w_part(n, k * P, (k + 1) * P), h_part(k, 0, SEQ), k == 0, k == KT - 1)
                    ins.then_inc(unit_full, 1)
                    if c == 0 and s == 0:
                        side(LAST_SIDE)
                n = GATE0 + 3 * c + 2
                wait_lo(pe, n)
                if c == 0:
                    pe.wait_ge(o_lo, 2 * TILES)
                for s, (hi, lo) in enumerate(((ob_hi, ob_lo), (oa_hi, oa_lo))[::-1]):
                    if c >= 2:
                        pe.wait_ge(sig_used, 2 * (c - 2) + s + 1)
                    bank = (qb if s == 0 else ob)[c % 2]
                    for k in range(KW):
                        ins = three(bank[:, :], w_part(n, (s * KW + k) * P, (s * KW + k + 1) * P),
                                    (hi[:, k, :], lo[:, k, :]), k == 0, k == KW - 1)
                    ins.then_inc(branch_full, 1)

            for m, (i, piece, cols) in enumerate(OUT_UNITS):
                wait_unit_read(pe, len(UNITS) + 2 * KT + m - 2)
                t = slice(i * P, (i + 1) * P)
                bank = pj[out_bank(m)][:, 0:cols.stop - cols.start]
                for k in range(KT):
                    if m == 0:
                        pe.wait_ge(m_lo_made, k + 1)
                        wait_lo(pe, OUT0 + k)
                    ins = three(bank, (m_hi[:, k, t], m_lo[:, k, t]), w_part(OUT0 + k, cols.start, cols.stop),
                                k == 0, k == KT - 1)
                ins.then_inc(unit_full, 1)


_INS = ["x", "norm_g", "w_in", "conv_w", "conv_b", "b_igate", "b_fgate", "head_norm_g",
        "w_branch_a", "w_branch_b", "w_out", "final_norm_g"]


def _rope_table():
    import numpy as np

    inv = np.float32(ROPE_THETA) ** (-(np.arange(HALF, dtype=np.float32) * np.float32(2.0) / np.float32(ROT)))
    ang = np.arange(SEQ, dtype=np.float32)[:, None] * inv.astype(np.float32)[None, :]
    cos, sin = np.cos(ang), np.sin(ang)
    return np.stack([np.concatenate([cos, cos], 1), np.concatenate([-sin, sin], 1)], 1).astype(np.float32)


def kernel(**inputs):
    import numpy as np
    import concourse.bacc as bacc
    from concourse.bass_utils import run_bass_kernel_spmd

    nc = bacc.Bacc("TRN2", target_bir_lowering=False, num_devices=1)
    arrays, args = {}, []

    def give(name, a):
        arrays[name] = a
        args.append(nc.dram_tensor(name, a.shape, mybir.dt.from_np(a.dtype), kind="ExternalInput").ap())

    for name in _INS:
        a = np.asarray(inputs[name])
        if name != "final_norm_g":
            a = a[0]
        if name in ("norm_g", "conv_b"):
            a = a.reshape(-1, P).T
        if name == "conv_w":
            a = a.reshape(CONV_WIDTH, -1, P).transpose(2, 1, 0)
        give(f"in_{name}", np.ascontiguousarray(a))
    give("const_ident", np.eye(P, dtype=np.float32))
    give("const_rope", _rope_table())
    args.append(nc.dram_tensor("out_0", (SEQ, D_MODEL), F32, kind="ExternalOutput").ap())
    hybrid_kernel(nc, *args)
    r = run_bass_kernel_spmd(nc, [arrays], core_ids=[0])
    return r.results[0]["out_0"].reshape(1, SEQ, D_MODEL)
```
